# Optimizing a Trainium2 kernel written in Bass

```python
import jax, jax.numpy as jnp
from jax import lax
import numpy as np

D_MODEL = 1024
BATCH = 1
SEQ = 2048
DEPTH = 1

CHUNK = 64
CONV_WIDTH = 3
D_CONV = D_MODEL
HEAD_DIM = 64
N_HEADS = D_MODEL // HEAD_DIM
D_RWKV = N_HEADS * HEAD_DIM
DECAY_RANK = 64
AAA_RANK = 64
VMIX_RANK = 32
GATE_RANK = 128
N_EXPERTS = 32
N_GROUPS = 8
EXPERTS_PER_GROUP = N_EXPERTS // N_GROUPS
TOP_K = 2
D_EXPERT = 512
M_BLK = 128
NORM_EPS = 1e-6
LN_X_EPS = 64e-5

N_PLAIN = 3 * D_CONV + 2 * D_MODEL
N_SHIFT = 3 * D_RWKV + DECAY_RANK + AAA_RANK + GATE_RANK
N_IN = N_PLAIN + N_SHIFT

kernel_name = 'hybrid_conv_rwkv7_grouped_moe_trunk'

def rms_norm(x, gain):
    x32 = x.astype(jnp.float32)
    y = x32 * lax.rsqrt(jnp.mean(x32 * x32, axis=-1, keepdims=True) + NORM_EPS)
    return (y * gain.astype(jnp.float32)).astype(x.dtype)

def token_shift(p):
    return jnp.pad(p, ((0, 0), (1, 0), (0, 0)))[:, :-1]

def causal_dwconv(u, w):
    s = u.shape[1]
    up = jnp.pad(u, ((0, 0), (CONV_WIDTH - 1, 0), (0, 0)))
    return sum(up[:, j:j + s] * w[j] for j in range(CONV_WIDTH))

def wkv7(r, decay, k, v, kk, a):
    bn, s = r.shape[0], r.shape[1]
    nc = s // CHUNK

    def to_chunks(t):
        return t.reshape(bn, nc, CHUNK, N_HEADS, HEAD_DIM).transpose(1, 2, 0, 3, 4)

    xs = (to_chunks(r), to_chunks(decay), to_chunks(k), to_chunks(v), to_chunks(kk), to_chunks(a))

    def step(state, inp):
        r_t, w_t, k_t, v_t, kk_t, a_t = inp
        sa = jnp.einsum('bhvk,bhk->bhv', state, kk_t)
        state = (state * w_t[:, :, None, :]
                 - sa[..., None] * (kk_t * a_t)[:, :, None, :]
                 + v_t[..., None] * k_t[:, :, None, :])
        y = jnp.einsum('bhvk,bhk->bhv', state, r_t)
        return state, y

    def chunk_step(state, chunk_inp):
        return lax.scan(step, state, chunk_inp)

    s0 = jnp.zeros((bn, N_HEADS, HEAD_DIM, HEAD_DIM), jnp.float32)
    _, y = lax.scan(chunk_step, s0, xs)
    return y.transpose(2, 0, 1, 3, 4).reshape(bn, s, N_HEADS, HEAD_DIM)

def heads(t):
    return t.reshape(t.shape[0], t.shape[1], N_HEADS, HEAD_DIM)

def token_mixer(h, v_first, w_in, token_mu, conv_w, w0, decay_up, a0, aaa_up, gate_up,
                k_k, k_a, r_k, ln_x_w, ln_x_b, vmix, w_out):
    bn, s, _ = h.shape
    p = h @ w_in
    plain, rw = p[..., :N_PLAIN], p[..., N_PLAIN:]
    rw = rw + (token_shift(rw) - rw) * token_mu

    cb, cc, ch, ga, gb = jnp.split(plain, [D_CONV, 2 * D_CONV, 3 * D_CONV, 3 * D_CONV + D_MODEL], axis=-1)
    y_conv = cb * causal_dwconv(cc * ch, conv_w)

    r, k, v, wd, ad, gd = jnp.split(
        rw, [D_RWKV, 2 * D_RWKV, 3 * D_RWKV, 3 * D_RWKV + DECAY_RANK, 3 * D_RWKV + DECAY_RANK + AAA_RANK], axis=-1)
    w_log = -jax.nn.softplus(-(w0 + jnp.tanh(wd) @ decay_up).astype(jnp.float32)) - 0.5
    decay = jnp.exp(-jnp.exp(w_log))
    a = jax.nn.sigmoid(a0 + ad @ aaa_up)
    g = jax.nn.sigmoid(gd) @ gate_up
    if vmix is None:
        v_first = v
    else:
        vmix_down, vmix_up, v0 = vmix
        v = v + (v_first - v) * jax.nn.sigmoid(v0 + (h @ vmix_down) @ vmix_up)
    kk = heads(k * k_k).astype(jnp.float32)
    kk = kk / jnp.maximum(jnp.sqrt(jnp.sum(kk * kk, axis=-1, keepdims=True)), 1e-12)
    k = k * (1.0 + (a - 1.0) * k_a)
    r_h = heads(r).astype(jnp.float32)
    k_h = heads(k).astype(jnp.float32)
    v_h = heads(v).astype(jnp.float32)
    a_h = heads(a).astype(jnp.float32)
    y = wkv7(r_h, heads(decay), k_h, v_h, kk, a_h)
    mu = jnp.mean(y, axis=-1, keepdims=True)
    var = jnp.mean(jnp.square(y - mu), axis=-1, keepdims=True)
    yn = ((y - mu) * lax.rsqrt(var + LN_X_EPS)).reshape(bn, s, D_RWKV)
    yn = yn * ln_x_w.astype(jnp.float32) + ln_x_b.astype(jnp.float32)
    bonus = jnp.sum(r_h * k_h * r_k.astype(jnp.float32), axis=-1, keepdims=True) * v_h
    y_rwkv = ((yn + bonus.reshape(bn, s, D_RWKV)) * g.astype(jnp.float32)).astype(h.dtype)

    merged = jax.nn.sigmoid(ga) * y_conv + jax.nn.sigmoid(gb) * y_rwkv
    return merged @ w_out, v_first

def moe(h, w_router, router_bias, w_e_in, w_e_out):
    bn, s, d = h.shape
    hf = h.reshape(bn * s, d)
    t = hf.shape[0]
    n_assign = t * TOP_K
    aff = jax.nn.sigmoid((hf @ w_router).astype(jnp.float32))
    sel = (aff + router_bias.astype(jnp.float32)).reshape(t, N_GROUPS, EXPERTS_PER_GROUP)
    gscore = jnp.sum(lax.top_k(sel, TOP_K)[0], axis=-1)
    gsel = jnp.argmax(gscore, axis=-1).astype(jnp.int32)
    cand = jnp.take_along_axis(sel, gsel[:, None, None], axis=1)[:, 0]
    _, local = lax.top_k(cand, TOP_K)
    eidx = gsel[:, None] * EXPERTS_PER_GROUP + local
    wts = jnp.take_along_axis(aff, eidx, axis=-1)
    wts = wts / jnp.sum(wts, axis=-1, keepdims=True)

    flat_e = eidx.reshape(n_assign)
    order = jnp.argsort(flat_e)
    sorted_e = flat_e[order]
    tok = order // TOP_K
    sizes = jnp.bincount(flat_e, length=N_EXPERTS)
    padded = (sizes + M_BLK - 1) // M_BLK * M_BLK
    pad_end = jnp.cumsum(padded)
    pad_start = pad_end - padded
    start = jnp.cumsum(sizes) - sizes
    dest = pad_start[sorted_e] + jnp.arange(n_assign) - start[sorted_e]
    n_rows = n_assign + N_EXPERTS * M_BLK
    n_blocks = n_rows // M_BLK
    buf = jnp.zeros((n_rows, d), h.dtype).at[dest].set(hf[tok])
    blk_e = jnp.minimum(jnp.searchsorted(pad_end, jnp.arange(n_blocks) * M_BLK, side='right'), N_EXPERTS - 1)

    def expert_block(args):
        xb, e = args
        gate, up = jnp.split(xb @ w_e_in[e], 2, axis=-1)
        return (jax.nn.silu(gate) * up) @ w_e_out[e]

    yb = lax.map(expert_block, (buf.reshape(n_blocks, M_BLK, d), blk_e))
    ye = yb.reshape(n_rows, d)[dest] * wts.reshape(n_assign)[order][:, None].astype(h.dtype)
    return jnp.zeros_like(hf).at[tok].add(ye).reshape(bn, s, d)

def setup_inputs(seed: int = 0) -> dict:
    key = jax.random.key(seed)
    ks = jax.random.split(key, 32)
    f32 = jnp.float32
    nrm = lambda k, shape, scale: jax.random.normal(k, shape, f32) * scale
    inv = lambda n: float(n) ** -0.5
    return {
        'x': nrm(ks[0], (BATCH, SEQ, D_MODEL), 1.0),
        'c': nrm(ks[1], (BATCH, D_MODEL), 1.0),
        'w_ada': nrm(ks[2], (DEPTH, D_MODEL, 6 * D_MODEL), 0.5 * inv(D_MODEL)),
        'b_ada': nrm(ks[3], (DEPTH, 6 * D_MODEL), 0.01),
        'norm1_gain': 1.0 + nrm(ks[4], (DEPTH, D_MODEL), 0.05),
        'norm2_gain': 1.0 + nrm(ks[5], (DEPTH, D_MODEL), 0.05),
        'w_in': nrm(ks[6], (DEPTH, D_MODEL, N_IN), inv(D_MODEL)),
        'token_mu': jax.random.uniform(ks[7], (DEPTH, N_SHIFT), f32),
        'conv_w': nrm(ks[8], (DEPTH, CONV_WIDTH, D_CONV), inv(CONV_WIDTH)),
        'w0': jnp.linspace(-6.0, -1.0, D_RWKV, dtype=f32)[None, :] + nrm(ks[9], (DEPTH, D_RWKV), 0.1),
        'decay_up': nrm(ks[10], (DEPTH, DECAY_RANK, D_RWKV), 0.1 * inv(DECAY_RANK)),
        'a0': nrm(ks[11], (DEPTH, D_RWKV), 0.1),
        'aaa_up': nrm(ks[12], (DEPTH, AAA_RANK, D_RWKV), 0.5 * inv(AAA_RANK)),
        'gate_up': nrm(ks[13], (DEPTH, GATE_RANK, D_RWKV), inv(GATE_RANK)),
        'k_k': 0.85 + nrm(ks[14], (DEPTH, D_RWKV), 0.05),
        'k_a': 1.0 + nrm(ks[15], (DEPTH, D_RWKV), 0.05),
        'r_k': nrm(ks[16], (DEPTH, N_HEADS, HEAD_DIM), 0.1),
        'ln_x_w': 1.0 + nrm(ks[17], (DEPTH, D_RWKV), 0.05),
        'ln_x_b': nrm(ks[18], (DEPTH, D_RWKV), 0.01),
        'vmix_down': nrm(ks[19], (DEPTH - 1, D_MODEL, VMIX_RANK), inv(D_MODEL)),
        'vmix_up': nrm(ks[20], (DEPTH - 1, VMIX_RANK, D_RWKV), inv(VMIX_RANK)),
        'v0': nrm(ks[21], (DEPTH - 1, D_RWKV), 0.1),
        'w_out': nrm(ks[22], (DEPTH, D_MODEL, D_MODEL), inv(D_MODEL)),
        'w_router': nrm(ks[23], (D_MODEL, N_EXPERTS), inv(D_MODEL)),
        'router_bias': nrm(ks[24], (N_EXPERTS,), 0.01),
        'w_expert_in': nrm(ks[25], (DEPTH, N_EXPERTS, D_MODEL, 2 * D_EXPERT), inv(D_MODEL)),
        'w_expert_out': nrm(ks[26], (DEPTH, N_EXPERTS, D_EXPERT, D_MODEL), inv(D_EXPERT)),
        'final_gain': 1.0 + nrm(ks[27], (D_MODEL,), 0.05),
    }

def reference(x, c, w_ada, b_ada, norm1_gain, norm2_gain, w_in, token_mu, conv_w, w0,
              decay_up, a0, aaa_up, gate_up, k_k, k_a, r_k, ln_x_w, ln_x_b,
              vmix_down, vmix_up, v0, w_out, w_router, router_bias,
              w_expert_in, w_expert_out, final_gain):
    v_first = None
    cond = jax.nn.silu(c)
    for l in range(DEPTH):
        ada = (cond @ w_ada[l] + b_ada[l])[:, None, :]
        sh1, sc1, g1, sh2, sc2, g2 = jnp.split(ada, 6, axis=-1)
        h = rms_norm(x, norm1_gain[l]) * (1.0 + sc1) + sh1
        vmix = None if l == 0 else (vmix_down[l - 1], vmix_up[l - 1], v0[l - 1])
        mix, v_first = token_mixer(h, v_first, w_in[l], token_mu[l], conv_w[l], w0[l], decay_up[l],
                                   a0[l], aaa_up[l], gate_up[l], k_k[l], k_a[l], r_k[l],
                                   ln_x_w[l], ln_x_b[l], vmix, w_out[l])
        x = x + g1 * mix
        h2 = rms_norm(x, norm2_gain[l]) * (1.0 + sc2) + sh2
        x = x + g2 * moe(h2, w_router, router_bias, w_expert_in[l], w_expert_out[l])
    return rms_norm(x, final_gain)


_drawn_inputs = setup_inputs


def setup_inputs(seed=0):
    import zlib

    import numpy as np

    out = dict(_drawn_inputs(seed))
    spreads = {}
    factors = {'decay_up': 8.0,
     'a0': 4.535,
     'k_k': 4.097,
     'k_a': 3.375,
     'ln_x_w': 3.959,
     'ln_x_b': 34.188}
    for name, (base, spread) in spreads.items():
        noise = np.random.default_rng([zlib.crc32(name.encode()), seed]).standard_normal(out[name].shape)
        drawn = base * np.exp(spread * noise) if base else spread * noise
        out[name] = __import__('jax').numpy.asarray(drawn.astype(out[name].dtype))
    for name, factor in factors.items():
        out[name] = (out[name] * factor).astype(out[name].dtype)
    return out
```

```python
import math
from contextlib import ExitStack

import concourse.bass as bass
from concourse import mybir

F32 = mybir.dt.float32
I32 = mybir.dt.int32
U32 = mybir.dt.uint32
ALU = mybir.AluOpType
ACT = mybir.ActivationFunctionType
AX = mybir.AxisListType
ds = bass.ds

P = 128
D = 1024
KT = D // P
T = 2048
G = 512
NG = T // G
C = 64
NC = G // C
STEPS = KT * NG
NTILE = T // P
HD = 64
NE = 32
NGRP = 8
EPG = NE // NGRP
DE = 512
NB = 64
EPS = 1e-6
LNX_EPS = 64e-5
DECAY_SCALE = -math.exp(-0.5)
TINY_SHIFT = 2.0 ** 30
N_PLAIN = 5 * D
RANK_COL = N_PLAIN + 3 * D

COLS = [("k", N_PLAIN + D), ("r", N_PLAIN), ("v", N_PLAIN + 2 * D), ("ch", 2 * D), ("cc", D), ("cb", 0),
        ("ga", 3 * D), ("gb", 4 * D)]
(Q_MUR, Q_MUK, Q_MUV, Q_KK, Q_KA, Q_A0, Q_W0, Q_RK, Q_LNW, Q_LNB, Q_CW0, Q_CW1, Q_CW2, Q_N1, Q_OMR, Q_OMK,
 Q_OMV, Q_OKA) = range(18)
NLOAD = 14
NQ = 18


def gram_plan():
    plan = []
    for b in range(2):
        plan += [("L", 0, b, 0), ("LT", 0, b, 0), ("LT", 0, b, 1)]
    fill = [("GK", 0, b, h) for b in range(2) for h in range(2)]
    fill += [("TR", m, b, 0) for m in range(3) for b in range(2)]
    for lv in range(1, 6):
        for b in range(2):
            plan.append(("Z", lv, b, 0))
        plan += fill[2 * (lv - 1):2 * lv]
        for b in range(2):
            if lv < 5:
                plan.append(("T", lv, b, 0))
            plan.append(("Q", lv, b, 0))
    return plan


PLAN = gram_plan()
NUSE = len(PLAN)
ON_ACT = [u for u in PLAN if u[0] == "TR"]
ON_DVE = [u for u in PLAN if u[0] != "TR"]


def build(nc, io, out):
    ctx = ExitStack()
    with ctx:
        names = """consts_ready c_sig cond_ready par_rows par_T par_ready ada_done ada_row ada_T mod_ready xn_ready rw_in
        parq_step rank_done rank_carry rank_scaled rank_mixed rank_out rank_saved cleared ups_in gate_in wa_in gd_in
        par_step zdec_done zaaa_done sgT_done cum_done norm_done center_done var_done gup_done bonus_done
        proj_done sg_ready a_ready carry_saved sgT_copied ksq_ready norm_max rk_ready rkbd_ready kk_ready
        b_ready V_written ch_copied u_carry u_made cb_gated x_done u_done s_done y_done x_copied u_copied
        S_updated S_init yT_copied merged_ready merged_out gram_done gram_evac T_seeded Q_half Q_seeded
        tok_copied wo_in bcast_rows bcast_done bcast_ready mix_done mixed x1_ready xn2_ready logit_done
        logit_copied aff_ready rank_mm tbl_out tbl_back tbl_T idx_ready dest_ready scat_out blk_ready
        gu_done sig_ready silu_ready act_ready actT_done actT_ready y2_done y_act y_dve y1w y12 y12g
        x2_ready o_ready shift_scaled shifted operands gates branch km_step rn_step P_step hats rs_step
        yc_step post_step conv_step sumsq ln_done rstd tr_done T_act T_dve index_col chain patterns
        ada_trip""".split()
        S = {n: ctx.enter_context(nc.semaphore(n)) for n in names}
        by_slot = "ada_w x_in mT_in x5_in x1_out xn2_out we_in xg_in y_out y8_in x8_in o_out".split()
        SL = {n: [ctx.enter_context(nc.semaphore(f"{n}{s}")) for s in range(2)] for n in by_slot}
        w_in_sem = [ctx.enter_context(nc.semaphore(f"w_{n}_in")) for n, _ in COLS]

        def sb(stack, name, shape, dt=F32):
            return stack.enter_context(nc.sbuf_tensor(name, shape, dt))

        def dram(name, shape, dt=F32):
            return nc.dram_tensor(name, shape, dt, kind="Internal").ap()

        rank_s = dram("rank_s", [2, P, T])
        merged_s = dram("merged_s", [D, T])
        x1_s = dram("x1_s", [T, D])
        xn2_s = dram("xn2_s", [T, D])
        ada_s = dram("ada_s", [48, P])
        tbl_s = dram("tbl_s", [NB * P, 1])
        y_s = dram("y_s", [NB * P, D])

        banks = [ctx.enter_context(nc.psum_tensor(f"bank{i}", [P, 512], F32)) for i in range(8)]
        PJ = banks[0:2]
        M0, M1 = banks[2], banks[3]
        SA, SB, SC, SD = banks[4], banks[5], banks[6], banks[7]
        RING = [SD, SA, SB, SC]

        ident = sb(ctx, "ident", [P, P])
        ones_bd = sb(ctx, "ones_bd", [P, P])
        center = sb(ctx, "center", [P, P])
        tri = sb(ctx, "tri", [P, P])
        mN = sb(ctx, "mN", [P, 192])
        m0n = sb(ctx, "m0n", [P, P])
        m0Tn = sb(ctx, "m0Tn", [P, P])
        mlev = sb(ctx, "mlev", [P, 5, P])
        PT = sb(ctx, "PT", [P, NQ, KT])
        PT2 = sb(ctx, "PT2", [P, 18])
        om2 = sb(ctx, "om2", [P, 2])
        adaT = sb(ctx, "adaT", [P, 48])
        modc = sb(ctx, "modc", [P, 4, KT])
        epsc = sb(ctx, "epsc", [P, 4])
        nz = sb(ctx, "nz", [P, NG])

        main = ctx.enter_context(ExitStack())

        p1 = ExitStack()
        rows1 = sb(p1, "rows1", [112, P])
        rows2 = sb(p1, "rows2", [18, P])
        brow = sb(p1, "brow", [1, 48 * P])
        csig = sb(p1, "csig", [P, KT])
        cond = sb(p1, "cond", [P, KT])
        adaw = sb(p1, "adaw", [P, 2, KT, 512])
        adarow = sb(p1, "adarow", [1, 48 * P])
        ada48 = sb(p1, "ada48", [48, P])
        iop = sb(p1, "iop", [P, P], I32)
        iof = sb(p1, "iof", [P, P], I32)
        xr = sb(p1, "xr", [P, P])
        low = sb(p1, "low", [P, P])
        upp = sb(p1, "upp", [P, P])
        lx = sb(p1, "lx", [P, P])
        ux = sb(p1, "ux", [P, P])
        geq = sb(p1, "geq", [P, 8, P])
        gequ = sb(p1, "gequ", [P, 3, P])

        p1.close()
        hT = sb(main, "hT", [P, KT, T])
        p2 = ExitStack()
        xt = sb(p2, "xt", [P, 2, D])
        xsq = sb(p2, "xsq", [P, D])
        xst = sb(p2, "xst", [P, 2, 4])
        p3 = ExitStack()
        wrank = sb(p3, "wrank", [P, KT, 256])
        rsc = sb(p3, "rsc", [P, 2, G + 1])
        rmx = sb(p3, "rmx", [P, 2, G])
        rout = sb(p3, "rout", [P, 2, G])
        p3.close()
        p2.close()

        p4 = ExitStack()
        w = sb(p4, "w", [P, 8, KT, P])
        UP = sb(p4, "UP", [P, 3, P])
        WAc = sb(p4, "WAc", [P, G])
        GDc = sb(p4, "GDc", [P, G])
        par = sb(p4, "par", [P, NQ])
        parQ = sb(p4, "parQ", [P, NQ])
        AR = sb(p4, "AR", [P, NC, 192])
        LTb = sb(p4, "LTb", [P, NC, 192])
        GKb = sb(p4, "GKb", [P, NC, 192])
        Tm = sb(p4, "Tm", [P, NC, P])
        Qm = sb(p4, "Qm", [P, NC, P])
        Zm = sb(p4, "Zm", [P, NC, P])
        Bb = sb(p4, "Bb", [P, NC, P])
        Kb = sb(p4, "Kb", [P, NC, P])
        Vb = sb(p4, "Vb", [P, NC, P])
        tok = sb(p4, "tok", [P, 3, NC, P])
        T3 = sb(p4, "T3", [P, 3, G + 1])
        kt = sb(p4, "kt", [P, G])
        rt = sb(p4, "rt", [P, G])
        vt = sb(p4, "vt", [P, G])
        Pb = sb(p4, "Pb", [P, NC, C + 1])
        Pinv = sb(p4, "Pinv", [P, G])
        sg = sb(p4, "sg", [P, G])
        at = sb(p4, "at", [P, G])
        km = sb(p4, "km", [P, G])
        kk = sb(p4, "kk", [P, G])
        sq = sb(p4, "sq", [P, G])
        ub = sb(p4, "ub", [P, G + 2])
        conv = sb(p4, "conv", [P, G])
        cg = sb(p4, "cg", [P, G])
        chs = sb(p4, "chs", [P, G])
        gg = sb(p4, "gg", [P, G])
        bv = sb(p4, "bv", [P, G])
        yT = sb(p4, "yT", [P, G])
        mg = sb(p4, "mg", [P, G])
        rkbd = sb(p4, "rkbd", [P, P])
        xs = sb(p4, "xs", [P, P])
        ut = sb(p4, "ut", [P, P])
        St = sb(p4, "St", [P, 2, P])
        pcs = sb(p4, "pcs", [P, NC])
        p4.close()
        main.close()
        rk = sg
        yc, rs = yT, sq
        sgT = Pinv
        rn = cg

        g1b = sb(ctx, "g1b", [P, D])
        g2b = sb(ctx, "g2b", [P, D])
        fgb = sb(ctx, "fgb", [P, D])
        biasb = sb(ctx, "biasb", [P, NE])
        aff = sb(ctx, "aff", [P, NTILE * NE])
        p5 = ExitStack()
        wo = sb(p5, "wo", [P, KT, D])
        mT = sb(p5, "mT", [P, 2, KT, P])
        x5 = sb(p5, "x5", [P, 2, D])
        x1t = sb(p5, "x1t", [P, 2, D])
        xn2 = sb(p5, "xn2", [P, 2, D])
        sq5 = sb(p5, "sq5", [P, D])
        st5 = sb(p5, "st5", [P, 2, 4])
        h2T = sb(p5, "h2T", [P, 2, KT, P])
        wr = sb(p5, "wr", [P, KT, NE])
        ones_row = sb(p5, "ones_row", [1, P])
        brow5 = sb(p5, "brow5", [1, 3 * D + NE])
        p5.close()

        dest = sb(ctx, "dest", [P, 2, NTILE], U32)
        wts = sb(ctx, "wts", [P, 2, NTILE])
        gate = sb(ctx, "gate", [P, 2])
        IDX = sb(ctx, "IDX", [P, NB], U32)
        blk = sb(ctx, "blk", [1, NB], I32)
        p6 = ExitStack()
        RW = NTILE * NE
        lg = [sb(p6, f"lg{i}", [P, RW]) for i in range(10)]
        s8 = [sb(p6, f"s8_{i}", [P, NTILE * NGRP]) for i in range(8)]
        s16 = [sb(p6, f"s16_{i}", [P, NTILE]) for i in range(6)]
        e32 = [sb(p6, f"e32_{i}", [P, 64]) for i in range(6)]
        e32i = sb(p6, "e32i", [P, NE], I32)
        revg = sb(p6, "revg", [P, NTILE * NGRP])
        reve = sb(p6, "reve", [P, RW])
        sut = sb(p6, "sut", [P, P])
        onesq = sb(p6, "onesq", [P, P])
        tid = sb(p6, "tid", [P, NTILE])
        tblz = sb(p6, "tblz", [NB, P])
        tblr = sb(p6, "tblr", [NB, P])
        bidx = sb(p6, "bidx", [1, NB, NE])
        bcmp = sb(p6, "bcmp", [1, NB, NE])
        bf = sb(p6, "bf", [1, NB])
        p6.close()

        p7 = ExitStack()
        WI = sb(p7, "WI", [P, 2, KT, 2 * DE])
        WO = sb(p7, "WO", [P, 2, DE // P, D])
        xg = sb(p7, "xg", [P, 2, D])
        idxs = sb(p7, "idxs", [P, 2], U32)
        xT = sb(p7, "xT", [P, 2, KT, P])
        gsig = sb(p7, "gsig", [P, 2, DE])
        actb = sb(p7, "actb", [P, 2, DE])
        aT = sb(p7, "aT", [P, 2, DE])
        ysb = sb(p7, "ysb", [P, 2, D])
        p7.close()

        p8 = ExitStack()
        ya = sb(p8, "ya", [P, 2, D])
        yb = sb(p8, "yb", [P, 2, D])
        x8 = sb(p8, "x8", [P, 2, D])
        c8 = sb(p8, "c8", [P, 2, D])
        o8 = sb(p8, "o8", [P, 2, D])
        sq8 = sb(p8, "sq8", [P, D])
        st8 = sb(p8, "st8", [P, 2, 4])
        dix = sb(p8, "dix", [P, 2, 2], U32)
        wdx = sb(p8, "wdx", [P, 2, 2])
        p8.close()

        block = ctx.enter_context(nc.Block())

        w_cols = io["w_in"].rearrange("l (k p) n -> p (l k) n", p=P)
        w_ada = io["w_ada"].rearrange("l (k p) n -> p (l k) n", p=P)
        w_out = io["w_out"].rearrange("l (k p) n -> p (l k) n", p=P)
        x_rows = io["x"].rearrange("b t d -> (b t) d")
        out_rows = out.rearrange("b t d -> (b t) d")

        def rows_of(ap):
            return ap.rearrange("l (r c) -> (l r) c", c=P)

        ada_row_s = ada_s.rearrange("a b -> (a b)").rearrange("(o n) -> o n", o=1)

        def last(i):
            return isinstance(i, int)

        e_in = io["w_expert_in"]
        e_out = io["w_expert_out"]

        def pairs(eng, body):
            for s in range(2):
                body(s, s)
            with eng.Fori(1, NTILE // 2) as h:
                for s in range(2):
                    body(h * 2 + s, s)

        def uses(n):
            return n // 2 + 1

        use_at = {u: n for n, u in enumerate(PLAN)}
        evac_at = {u: n for n, u in enumerate(ON_DVE)}
        tok_at = {u: n for n, u in enumerate(ON_ACT)}
        NDV, NTK = len(ON_DVE), len(ON_ACT)

        def wait_gram(eng, i, u):
            eng.wait_ge(S["gram_done"], i * NUSE + use_at[u] + 1)

        def wait_evac(eng, i, u):
            if u in evac_at:
                eng.wait_ge(S["gram_evac"], i * NDV + evac_at[u] + 1)
            else:
                eng.wait_ge(S["tok_copied"], i * NTK + tok_at[u] + 1)

        def bank(u):
            return RING[use_at[u] % 4]

        def first(i):
            return isinstance(i, int) and i == 0

        def group(i):
            return i % NG

        @block.sync
        def _(sp):
            mu = rows_of(io["token_mu"])
            plain = [mu[0:8, :], mu[8:16, :], mu[16:24, :], rows_of(io["k_k"]), rows_of(io["k_a"]),
                     rows_of(io["a0"]), rows_of(io["w0"]), io["r_k"].rearrange("l (r a) n -> (l r) (a n)", a=2),
                     rows_of(io["ln_x_w"]), rows_of(io["ln_x_b"])]
            plain += [io["conv_w"][:, j, :].rearrange("l (r c) -> (l r) c", c=P) for j in range(3)]
            plain += [rows_of(io["norm1_gain"])]
            for q, rows in enumerate(plain):
                sp.dma_start(rows1[8 * q:8 * q + 8, :], rows).then_inc(S["par_rows"], 16)
            sp.dma_start(rows2[0:8, :], rows_of(io["norm2_gain"])).then_inc(S["par_rows"], 16)
            sp.dma_start(rows2[8:10, :], mu[24:26, :]).then_inc(S["par_rows"], 16)
            sp.dma_start(rows2[10:18, :], rows_of(io["c"])).then_inc(S["par_rows"], 16)
            sp.dma_start(brow[0:1, :], io["b_ada"]).then_inc(S["par_rows"], 16)
            for n in range(12):
                if n >= 2:
                    sp.wait_ge(S["ada_done"], n - 1)
                sp.dma_start(adaw[:, n % 2], w_ada[:, :, 512 * n:512 * n + 512]).then_inc(SL["ada_w"][n % 2], 16)
            sp.wait_ge(S["ada_row"], 12)
            sp.dma_start(ada_row_s, adarow[0:1, :]).then_inc(S["ada_trip"], 16)
            sp.wait_ge(S["ada_trip"], 16)
            sp.dma_start(ada48[:, :], ada_s).then_inc(S["ada_trip"], 16)

            sp.wait_ge(S["mod_ready"], 1)
            sp.wait_ge(S["par_ready"], 1)
            sp.wait_ge(S["consts_ready"], 1)

            def load_x(n, s):
                if not last_pair_free(n):
                    sp.wait_ge(S["tr_done"], (n - 2) * 2 + 2)
                sp.dma_start(xt[:, s], x_rows[ds(n * P, P), :]).then_inc(SL["x_in"][s], 16)

            def last_pair_free(n):
                return isinstance(n, int)

            pairs(sp, load_x)

            sp.wait_ge(S["tr_done"], 2 * NTILE)
            sp.dma_start(wrank[:, :, :], w_cols[:, :, RANK_COL:RANK_COL + 256]).then_inc(S["rw_in"], 16)
            for g in range(NG):
                sp.wait_ge(S["rank_out"], 2 * g + 2)
                for m in range(2):
                    sp.dma_start(rank_s[m, :, G * g:G * g + G], rout[:, m]).then_inc(S["rank_saved"], 16)
            sp.wait_ge(S["rank_saved"], 32 * NG)

            def load_col(j, ct):
                sp.dma_start(w[:, j], w_cols[:, :, ds(ct * P + COLS[j][1], P)]).then_inc(w_in_sem[j], 16)

            def load_ups(ct):
                sp.dma_start(UP[0:64, 0, :], io["decay_up"][0, :, ds(ct * P, P)]).then_inc(S["ups_in"], 16)
                sp.dma_start(UP[64:128, 1, :], io["aaa_up"][0, :, ds(ct * P, P)]).then_inc(S["ups_in"], 16)

            def load_gate(ct):
                sp.dma_start(UP[:, 2, :], io["gate_up"][0, :, ds(ct * P, P)]).then_inc(S["gate_in"], 16)

            load_ups(0)
            sp.dma_start(WAc[:, :], rank_s[0, :, 0:G]).then_inc(S["wa_in"], 16)
            for j in range(8):
                load_col(j, 0)
                if j == 1:
                    load_gate(0)
                    sp.dma_start(GDc[:, :], rank_s[1, :, 0:G]).then_inc(S["gd_in"], 16)

            def load_step(ct, g, final=False):
                i = ct * NG + g
                nxt = (g + 1) % NG
                turn = g == NG - 1 and not final
                if not final:
                    sp.wait_ge(S["zaaa_done"], i + 1)
                    if turn:
                        load_ups(ct + 1)
                    sp.dma_start(WAc[:, :], rank_s[0, :, nxt * G:nxt * G + G]).then_inc(S["wa_in"], 16)
                if turn:
                    for j in range(6):
                        sp.wait_ge(S["proj_done"], i * 8 + j + 1)
                        load_col(j, ct + 1)
                if not first(i):
                    sp.wait_ge(S["merged_ready"], i)
                    pct, pg = (ct, g - 1) if g else (ct - 1, NG - 1)
                    sp.dma_start(merged_s[ds(pct * P, P), pg * G:pg * G + G], mg[:, :]).then_inc(S["merged_out"], 16)
                if not final:
                    sp.wait_ge(S["gup_done"], i + 1)
                    if turn:
                        load_gate(ct + 1)
                    sp.dma_start(GDc[:, :], rank_s[1, :, nxt * G:nxt * G + G]).then_inc(S["gd_in"], 16)
                if turn:
                    for j in (6, 7):
                        sp.wait_ge(S["proj_done"], i * 8 + j + 1)
                        load_col(j, ct + 1)

            for g in range(NG):
                load_step(0, g)
            with sp.Fori(1, KT - 1) as ct:
                for g in range(NG):
                    load_step(ct, g)
            for g in range(NG):
                load_step(KT - 1, g, final=g == NG - 1)
            sp.wait_ge(S["merged_ready"], STEPS)
            sp.dma_start(merged_s[(KT - 1) * P:, (NG - 1) * G:], mg[:, :]).then_inc(S["merged_out"], 16)

            sp.wait_ge(S["merged_out"], 16 * STEPS)
            sp.dma_start(wo[:, :, :], w_out).then_inc(S["wo_in"], 16)
            sp.dma_start(wr[:, :, :], io["w_router"].rearrange("(k p) e -> p k e", p=P)).then_inc(S["wo_in"], 16)
            sp.dma_start(brow5[0:1, 0:D], ada_row_s[:, 2 * D:3 * D]).then_inc(S["bcast_rows"], 16)
            sp.dma_start(brow5[0:1, D:2 * D], ada_row_s[:, 5 * D:6 * D]).then_inc(S["bcast_rows"], 16)
            sp.dma_start(brow5[0:1, 2 * D:3 * D], io["final_gain"].rearrange("(o n) -> o n", o=1))\
                .then_inc(S["bcast_rows"], 16)
            sp.dma_start(brow5[0:1, 3 * D:3 * D + NE], io["router_bias"].rearrange("(o n) -> o n", o=1))\
                .then_inc(S["bcast_rows"], 16)
            mview = merged_s.rearrange("(k p) t -> p k t", p=P)

            def load5(n, s):
                if not (isinstance(n, int) and n < 2):
                    sp.wait_ge(S["mix_done"], n - 1)
                    sp.wait_ge(S["x1_ready"], n - 1)
                sp.dma_start(mT[:, s], mview[:, :, ds(n * P, P)]).then_inc(SL["mT_in"][s], 16)
                sp.dma_start(x5[:, s], x_rows[ds(n * P, P), :]).then_inc(SL["x5_in"][s], 16)

            def store5(n, s):
                sp.wait_ge(S["x1_ready"], n + 1)
                sp.dma_start(x1_s[ds(n * P, P), :], x1t[:, s]).then_inc(SL["x1_out"][s], 16)
                sp.wait_ge(S["xn2_ready"], n + 1)
                sp.dma_start(xn2_s[ds(n * P, P), :], xn2[:, s]).then_inc(SL["xn2_out"][s], 16)

            load5(0, 0)
            load5(1, 1)
            with sp.Fori(1, NTILE // 2) as h:
                for s in range(2):
                    store5(h * 2 + s - 2, s)
                    load5(h * 2 + s, s)
            for s in range(2):
                store5(NTILE - 2 + s, s)

            sp.wait_ge(S["patterns"], 11)
            sp.dma_start(tbl_s.rearrange("(b p) o -> b (p o)", p=P), tblz[:, :]).then_inc(S["tbl_out"], 16)
            sp.wait_ge(S["scat_out"], 16 * 2 * NTILE)
            sp.dma_start(tblr[:, :], tbl_s.rearrange("(b p) o -> b (p o)", p=P)).then_inc(S["tbl_back"], 16)

            sp.wait_ge(S["idx_ready"], 1)
            sp.wait_ge(S["blk_ready"], 1)

            def load_expert(n, s):
                if not (isinstance(n, int) and n < 2):
                    sp.wait_ge(S["y2_done"], n - 1)
                e = sp.value_load(blk[0:1, ds(n, 1)], min_val=0, max_val=NE - 1)
                sp.dma_start(WI[:, s], e_in[0, ds(e, 1), :, :].rearrange("e (k p) n -> p (e k) n", p=P))\
                    .then_inc(SL["we_in"][s], 16)
                sp.dma_start(WO[:, s], e_out[0, ds(e, 1), :, :].rearrange("e (k p) n -> p (e k) n", p=P))\
                    .then_inc(SL["we_in"][s], 16)

            def store_y(n, s):
                sp.wait_ge(S["y_act"], n + 1)
                sp.wait_ge(S["y_dve"], n + 1)
                sp.dma_start(y_s[ds(n * P, P), :], ysb[:, s]).then_inc(SL["y_out"][s], 16)

            load_expert(0, 0)
            load_expert(1, 1)
            with sp.Fori(1, NB // 2) as h:
                for s in range(2):
                    load_expert(h * 2 + s, s)
                    store_y(h * 2 + s - 2, s)
            for s in range(2):
                store_y(NB - 2 + s, s)

            def load8(n, s):
                if not (isinstance(n, int) and n < 2):
                    sp.wait_ge(S["x2_ready"], n - 1)
                sp.dma_start(x8[:, s], x1_s[ds(n * P, P), :]).then_inc(SL["x8_in"][s], 16)

            def store8(n, s):
                sp.wait_ge(S["o_ready"], n + 1)
                sp.dma_start(out_rows[ds(n * P, P), :], o8[:, s]).then_inc(SL["o_out"][s], 16)

            for s in range(2):
                sp.wait_ge(SL["y_out"][s], 16 * NB // 2)
            load8(0, 0)
            load8(1, 1)
            with sp.Fori(1, NTILE // 2) as h:
                for s in range(2):
                    store8(h * 2 + s - 2, s)
                    load8(h * 2 + s, s)
            for s in range(2):
                store8(NTILE - 2 + s, s)
            for s in range(2):
                sp.wait_ge(SL["o_out"][s], 16 * NTILE // 2)

        @block.gpsimd
        def _(pool):
            nc.gpsimd.memset(ident[:, :], 0.0).then_inc(S["patterns"], 1)
            nc.gpsimd.memset(low[:, :], 1.0).then_inc(S["patterns"], 1)
            nc.gpsimd.memset(upp[:, :], 1.0).then_inc(S["patterns"], 1)
            nc.gpsimd.iota(iop[:, :], pattern=[[0, P]], base=0, channel_multiplier=1).then_inc(S["patterns"], 1)
            nc.gpsimd.iota(iof[:, :], pattern=[[1, P]], base=0, channel_multiplier=0).then_inc(S["patterns"], 1)
            pool.wait_ge(S["patterns"], 5)
            nc.gpsimd.affine_select(out=ident[:, :], in_=ident[:, :], compare_op=ALU.not_equal, fill=1.0, base=0,
                                    pattern=[[-1, P]], channel_multiplier=1).then_inc(S["patterns"], 1)
            nc.gpsimd.affine_select(out=low[:, :], in_=low[:, :], compare_op=ALU.is_gt, fill=0.0, base=0,
                                    pattern=[[-1, P]], channel_multiplier=1).then_inc(S["patterns"], 1)
            nc.gpsimd.affine_select(out=upp[:, :], in_=upp[:, :], compare_op=ALU.is_gt, fill=0.0, base=0,
                                    pattern=[[1, P]], channel_multiplier=-1).then_inc(S["patterns"], 1)

            for s in range(2):
                pool.wait_ge(SL["xn2_out"][s], 16 * NTILE // 2)
                pool.wait_ge(SL["x1_out"][s], 16 * NTILE // 2)
            pool.wait_ge(S["logit_copied"], NTILE)
            nc.gpsimd.iota(revg[:, :].rearrange("p (n g) -> p n g", g=NGRP), pattern=[[0, NTILE], [-1, NGRP]],
                           base=NGRP, channel_multiplier=0, allow_small_or_imprecise_dtypes=True).then_inc(S["patterns"], 1)
            nc.gpsimd.iota(reve[:, :].rearrange("p (n e) -> p n e", e=NE), pattern=[[0, NTILE], [-1, NE]],
                           base=NE, channel_multiplier=0, allow_small_or_imprecise_dtypes=True).then_inc(S["patterns"], 1)
            nc.gpsimd.memset(tblz[:, :], 0.0).then_inc(S["patterns"], 1)
            nc.gpsimd.iota(tid[:, :], pattern=[[P, NTILE]], base=0, channel_multiplier=1,
                           allow_small_or_imprecise_dtypes=True).then_inc(S["patterns"], 1)
            nc.gpsimd.iota(bidx[0:1, :, :], pattern=[[1, NB], [0, NE]], base=0, channel_multiplier=0,
                           allow_small_or_imprecise_dtypes=True).then_inc(S["patterns"], 1)
            nc.gpsimd.memset(sut[:, :], 1.0).then_inc(S["patterns"], 1)
            nc.gpsimd.memset(onesq[:, :], 1.0).then_inc(S["patterns"], 1)
            pool.wait_ge(S["patterns"], 15)
            nc.gpsimd.affine_select(out=sut[:, :], in_=sut[:, :], compare_op=ALU.is_gt, fill=0.0, base=0,
                                    pattern=[[1, P]], channel_multiplier=-1).then_inc(S["patterns"], 1)
            pool.wait_ge(S["dest_ready"], 1)
            pool.wait_ge(S["tbl_out"], 16)
            for n in range(NTILE):
                for j in range(2):
                    pool.indirect_dma_start(out=tbl_s, out_offset=bass.IndirectOffsetOnAxis(dest[:, j, n:n + 1], 0),
                                            in_=tid[:, n:n + 1], in_offset=None).then_inc(S["scat_out"], 16)

            nc.gpsimd.memset(gate[:, :], 0.0).then_inc(S["patterns"], 1)
            pool.wait_ge(S["patterns"], 17)
            pool.wait_ge(S["idx_ready"], 1)
            for s in range(2):
                pool.wait_ge(SL["xn2_out"][s], 16 * NTILE // 2)

            def gather(n, s):
                if not (isinstance(n, int) and n < 2):
                    pool.wait_ge(SL["xg_in"][s], (n // 2) * 16)
                    pool.wait_ge(S["tr_done"], 4 * NTILE + (n - 1) * 2)
                nc.gpsimd.tensor_copy(idxs[:, s:s + 1], IDX[:, ds(n, 1)]).then_inc(S["index_col"], 1)
                pool.wait_ge(S["index_col"], n + 1)
                nc.gpsimd.tensor_tensor(gate[:, 0:1], gate[:, 1:2], gate[:, 1:2], ALU.add)
                pool.indirect_dma_start(out=xg[:, s], out_offset=None, in_=xn2_s,
                                        in_offset=bass.IndirectOffsetOnAxis(idxs[:, s:s + 1], 0))\
                    .then_inc(SL["xg_in"][s], 16)

            gather(0, 0)
            gather(1, 1)
            with pool.Fori(1, NB // 2) as h:
                for s in range(2):
                    gather(h * 2 + s, s)

            for s in range(2):
                pool.wait_ge(SL["y_out"][s], 16 * NB // 2)

            def gather8(n, s):
                if not (isinstance(n, int) and n < 2):
                    pool.wait_ge(S["y12"], n - 1)
                    pool.wait_ge(S["index_col"], NB + n - 1)
                nc.gpsimd.tensor_copy(dix[:, s, :], dest[:, :, ds(n, 1)].rearrange("p a b -> p (a b)"))\
                    .then_inc(S["index_col"], 1)
                pool.wait_ge(S["index_col"], NB + n + 1)
                nc.gpsimd.tensor_tensor(gate[:, 0:1], gate[:, 1:2], gate[:, 1:2], ALU.add)
                pool.indirect_dma_start(out=ya[:, s], out_offset=None, in_=y_s,
                                        in_offset=bass.IndirectOffsetOnAxis(dix[:, s, 0:1], 0))\
                    .then_inc(SL["y8_in"][s], 16)
                pool.indirect_dma_start(out=yb[:, s], out_offset=None, in_=y_s,
                                        in_offset=bass.IndirectOffsetOnAxis(dix[:, s, 1:2], 0))\
                    .then_inc(SL["y8_in"][s], 16)

            gather8(0, 0)
            gather8(1, 1)
            with pool.Fori(1, NTILE // 2) as h:
                for s in range(2):
                    gather8(h * 2 + s, s)

        @block.tensor
        def _(pe):
            mm, tr = nc.tensor.matmul, nc.tensor.transpose

            pe.wait_ge(S["patterns"], 6)
            pe.wait_ge(S["par_rows"], 16 * 18)
            tr(PJ[0][:, 0:112], rows1[:, :], ident[0:112, 0:112])
            tr(PJ[1][:, 0:18], rows2[:, :], ident[0:18, 0:18]).then_inc(S["par_T"], 1)
            pe.wait_ge(S["cond_ready"], 1)
            for n in range(12):
                pe.wait_ge(SL["ada_w"][n % 2], 16 * (n // 2 + 1))
                if n >= 2:
                    pe.wait_ge(S["ada_row"], n - 1)
                bk = (M0, M1)[n % 2]
                for k in range(KT):
                    ins = mm(bk[0:1, :], cond[:, k:k + 1], adaw[:, n % 2, k, :], start=k == 0, stop=k == KT - 1)
                ins.then_inc(S["ada_done"], 1)
            pe.wait_ge(S["ada_trip"], 32)
            tr(SA[:, 0:48], ada48[:, :], ident[0:48, 0:48]).then_inc(S["ada_T"], 1)

            def transpose_x(n, s):
                pe.wait_ge(S["xn_ready"], n + 1)
                if not first(n):
                    pe.wait_ge(S["T_act"], n)
                for k in range(4):
                    ins = tr(PJ[0][:, k * P:k * P + P], xt[:, s, k * P:k * P + P], ident[:, :])
                ins.then_inc(S["tr_done"], 1)
                if not first(n):
                    pe.wait_ge(S["T_dve"], n)
                for k in range(4, 8):
                    ins = tr(PJ[1][:, (k - 4) * P:(k - 3) * P], xt[:, s, k * P:k * P + P], ident[:, :])
                ins.then_inc(S["tr_done"], 1)

            pairs(pe, transpose_x)

            pe.wait_ge(S["rw_in"], 16)
            pe.wait_ge(S["T_act"], NTILE)
            pe.wait_ge(S["T_dve"], NTILE)
            for g in range(NG):
                for m in range(2):
                    if g:
                        pe.wait_ge(S["rank_mixed"], 2 * (g - 1) + m + 1)
                    for k in range(KT):
                        ins = mm((M0, M1)[m][:, :], wrank[:, k, m * P:m * P + P], hT[:, k, g * G:g * G + G],
                                 start=k == 0, stop=k == KT - 1)
                    ins.then_inc(S["rank_done"], 1)

            def tile_no(i):
                return i // NG

            def zdec(i):
                pe.wait_ge(S["wa_in"], i * 16 + 16)
                pe.wait_ge(S["ups_in"], tile_no(i) * 32 + 32)
                if not first(i):
                    pe.wait_ge(S["branch"], i * 3)
                mm(M0[:, :], UP[:, 0, :], WAc[:, :], start=True, stop=True).then_inc(S["zdec_done"], 1)

            def zaaa(i):
                if not first(i):
                    pe.wait_ge(S["branch"], i * 3 - 1)
                mm(M1[:, :], UP[:, 1, :], WAc[:, :], start=True, stop=True).then_inc(S["zaaa_done"], 1)

            def sg_transposes(i):
                pe.wait_ge(S["sg_ready"], i + 1)
                for j in range(4):
                    ins = tr(M0[:, j * P:j * P + P], sg[:, j * P:j * P + P], ident[:, :])
                ins.then_inc(S["sgT_done"], 1)

            def cum(i):
                pe.wait_ge(S["sgT_copied"], i + 1)
                pe.wait_ge(S["a_ready"], i + 1)
                for j in range(4):
                    ins = mm(M1[:, j * P:j * P + P], sgT[:, j * P:j * P + P], tri[:, :], start=True, stop=True)
                ins.then_inc(S["cum_done"], 1)

            def norm(i):
                pe.wait_ge(S["ksq_ready"], i + 1)
                mm(M0[:, :], ones_bd[:, :], sq[:, :], start=True, stop=True).then_inc(S["norm_done"], 1)

            def gup(i):
                pe.wait_ge(S["gd_in"], i * 16 + 16)
                pe.wait_ge(S["gate_in"], tile_no(i) * 16 + 16)
                if first(i):
                    pe.wait_ge(S["P_step"], 2)
                else:
                    pe.wait_ge(S["yc_step"], i * 2)
                mm(M1[:, :], UP[:, 2, :], GDc[:, :], start=True, stop=True).then_inc(S["gup_done"], 1)

            def bonus(i):
                pe.wait_ge(S["rk_ready"], i + 1)
                pe.wait_ge(S["rkbd_ready"], i + 1)
                if first(i):
                    pe.wait_ge(S["norm_max"], 1)
                else:
                    pe.wait_ge(S["rs_step"], i * 2 - 1)
                mm(M0[:, :], rkbd[:, :], rk[:, :], start=True, stop=True).then_inc(S["bonus_done"], 1)

            def centred(q):
                pe.wait_ge(S["yT_copied"], q + 1)
                mm(M1[:, :], center[:, :], yT[:, :], start=True, stop=True).then_inc(S["center_done"], 1)

            def variance(q):
                pe.wait_ge(S["yc_step"], q * 2 + 2)
                mm(M0[:, :], ones_bd[:, :], sq[:, :], start=True, stop=True).then_inc(S["var_done"], 1)

            released = [(S["shifted"], 3, 1), (S["shifted"], 3, 2), (S["shifted"], 3, 3), (S["ch_copied"], 1, 1), (S["u_made"], 1, 1),
                        (S["cb_gated"], 1, 1), (S["gates"], 2, 1), (S["gates"], 2, 2)]

            def wait_released(j, i):
                signal, per_step, nth = released[j]
                pe.wait_ge(signal, i * per_step + nth)

            def proj(i, j, between):
                pe.wait_ge(w_in_sem[j], tile_no(i) * 16 + 16)
                if j >= 2:
                    wait_released(j - 2, i)
                elif not first(i):
                    wait_released(j + 6, i - 1)
                for k in range(KT):
                    ins = mm(PJ[j % 2][:, :], w[:, j, k, :], hT[:, k, ds(group(i) * G, G)],
                             start=k == 0, stop=k == KT - 1)
                    if k == KT - 1:
                        ins.then_inc(S["proj_done"], 1)
                    if k in between:
                        between[k]()

            def seq_x(q, c):
                if c == 0:
                    pe.wait_ge(S["S_init"], q + 1)
                    pe.wait_ge(S["gram_evac"], q * NDV + NDV)
                    pe.wait_ge(S["tok_copied"], q * NTK + NTK)
                    pe.wait_ge(S["Q_seeded"], q * 2 + 2)
                else:
                    pe.wait_ge(S["S_updated"], q * NC + c)
                    pe.wait_ge(S["u_copied"], q * NC + c)
                mm(SA[:, 0:P], GKb[:, c, 64:192], tok[:, 0, c, :], start=True, stop=False)
                mm(SA[:, 0:P], AR[:, c, 64:192], St[:, c % 2, :], start=False, stop=True).then_inc(S["x_done"], 1)

            def seq_u(q, c):
                pe.wait_ge(S["x_copied"], q * NC + c + 1)
                mm(SA[:, 0:P], Qm[:, c, :], xs[:, :], start=True, stop=True).then_inc(S["u_done"], 1)

            def seq_sy(q, c):
                pe.wait_ge(S["u_copied"], q * NC + c + 1)
                if c:
                    pe.wait_ge(S["S_updated"], q * NC + c)
                mm(SB[:, 0:P], tok[:, 2, c, :], tok[:, 0, c, :], start=True, stop=False)
                mm(SB[:, 0:P], tok[:, 1, c, :], ut[:, :], start=False, stop=True).then_inc(S["s_done"], 1)
                n = 128 if c < NC - 1 else 64
                y = SC[:, c * C:c * C + n]
                mm(y, tok[:, 0, c, :], GKb[:, c, 0:n], start=True, stop=False)
                mm(y, ut[:, :], LTb[:, c, 0:n], start=False, stop=False)
                mm(y, St[:, c % 2, :], AR[:, c, 0:n], start=False, stop=True).then_inc(S["y_done"], 1)

            def seq_hooks(q, c):
                if q is None:
                    return {}
                return {0: lambda: seq_x(q, c), 2: lambda: seq_u(q, c), 4: lambda: seq_sy(q, c),
                        5: lambda: seq_x(q, c + 1), 6: lambda: seq_u(q, c + 1), 7: lambda: seq_sy(q, c + 1)}

            def operands_of(kind, lv, b):
                if kind == "Z":
                    return [("LT", 0, b, 1)] if lv == 1 else [("T", lv - 1, b, 0)]
                if kind == "T":
                    return [("Z", lv, b, 0)] + ([("Q", lv - 1, b, 0)] if lv > 1 else [])
                if kind == "Q":
                    return [("Z", lv, b, 0)] + ([("Q", lv - 1, b, 0)] if lv > 1 else [])
                return []

            def grams(i):
                pe.wait_ge(S["operands"], i * 5 + 4)
                for n, u in enumerate(PLAN):
                    kind, lv, b, h = u
                    bk = bank(u)
                    reads = operands_of(kind, lv, b) + ([PLAN[n - 4]] if n >= 4 else [])
                    for engines in (evac_at, tok_at):
                        mine = [r for r in reads if r in engines]
                        if mine:
                            wait_evac(pe, i, max(mine, key=lambda r: use_at[r]))
                    if n < 4 and not first(i):
                        if n == 0:
                            pe.wait_ge(S["gram_evac"], i * NDV)
                        else:
                            pe.wait_ge((S["u_copied"], S["S_updated"], S["yT_copied"])[n - 1], i * (NC, NC, 1)[n - 1])
                    if kind == "L":
                        for c in range(4 * b, 4 * b + 4):
                            ins = mm(bk[:, (c % 4) * P:(c % 4) * P + P], AR[:, c, 64:192], Bb[:, c, :],
                                     start=True, stop=True)
                    elif kind in ("LT", "GK"):
                        if u == ("GK", 0, 0, 0):
                            pe.wait_ge(S["operands"], i * 5 + 5)
                        for z in range(2):
                            c = 4 * b + 2 * h + z
                            ins = mm(bk[:, z * 192:z * 192 + 192], (Bb if kind == "LT" else Kb)[:, c, :],
                                     AR[:, c, :], start=True, stop=True)
                    elif kind == "TR":
                        if b == 0:
                            pe.wait_ge((S["V_written"], S["hats"], S["hats"])[lv], (i + 1, i * 2 + 1, i * 2 + 2)[lv])
                        for c in range(4 * b, 4 * b + 4):
                            ins = tr(bk[:, (c % 4) * P:(c % 4) * P + P], (Vb, Bb, Kb)[lv][:, c, :], ident[:, :])
                    else:
                        if (kind, lv) == ("Z", 1):
                            pe.wait_ge(S["T_seeded"], i * 2 + b + 1)
                        if (kind, lv) == ("T", 1):
                            pe.wait_ge(S["Q_seeded"], i * 2 + b + 1)
                        left, right = {"Z": (LTb, Tm), "T": (Qm, Zm), "Q": (Zm, Qm)}[kind]
                        for c in range(4 * b, 4 * b + 4):
                            ins = mm(bk[:, (c % 4) * P:(c % 4) * P + P],
                                     left[:, c, 64:192] if kind == "Z" else left[:, c, :], right[:, c, :],
                                     start=True, stop=True)
                    ins.then_inc(S["gram_done"], 1)

            def step(i, q):
                zdec(i)
                zaaa(i)
                proj(i, 0, seq_hooks(q, 0))
                sg_transposes(i)
                proj(i, 1, seq_hooks(q, 2))
                cum(i)
                norm(i)
                proj(i, 2, seq_hooks(q, 4))
                proj(i, 3, seq_hooks(q, 6))
                proj(i, 4, {})
                if q is not None:
                    centred(q)
                proj(i, 5, {})
                if q is not None:
                    variance(q)
                proj(i, 6, {})
                gup(i)
                proj(i, 7, {})
                bonus(i)
                grams(i)

            pe.wait_ge(S["cleared"], 8)
            step(0, None)
            with pe.Fori(1, STEPS) as i:
                step(i, i - 1)
            for c in range(NC):
                seq_x(STEPS - 1, c)
                seq_u(STEPS - 1, c)
                seq_sy(STEPS - 1, c)
            pe.wait_ge(S["branch"], STEPS * 3 - 1)
            centred(STEPS - 1)
            pe.wait_ge(S["branch"], STEPS * 3)
            variance(STEPS - 1)

            pe.wait_ge(S["bcast_rows"], 64)
            pe.wait_ge(S["cleared"], 9)
            pe.wait_ge(S["yc_step"], STEPS * 2)
            pe.wait_ge(S["rs_step"], STEPS * 2 - 1)
            for n in range(7):
                wd = 512 if n < 6 else NE
                if n >= 2:
                    pe.wait_ge(S["bcast_ready"], n - 1)
                mm(PJ[n % 2][:, 0:wd], ones_row[0:1, :], brow5[0:1, 512 * n:512 * n + wd], start=True, stop=True)\
                    .then_inc(S["bcast_done"], 1)
            pe.wait_ge(S["bcast_ready"], 7)
            pe.wait_ge(S["wo_in"], 32)

            def out_product(n, s):
                pe.wait_ge(SL["mT_in"][s], uses(n) * 16)
                if not (isinstance(n, int) and n < 2):
                    pe.wait_ge(S["mixed"], n - 1)
                for j in range(2):
                    for k in range(KT):
                        ins = mm(banks[2 * s + j][:, :], mT[:, s, k, :], wo[:, k, j * 512:j * 512 + 512],
                                 start=k == 0, stop=k == KT - 1)
                ins.then_inc(S["mix_done"], 1)

            def router(n, s):
                pe.wait_ge(S["xn2_ready"], n + 1)
                for half in range(2):
                    if not first(n):
                        pe.wait_ge((S["T_act"], S["T_dve"])[half], NTILE + n)
                    for k in range(4):
                        kk_ = 4 * half + k
                        ins = tr((SA, SB)[half][:, k * P:k * P + P], xn2[:, s, kk_ * P:kk_ * P + P], ident[:, :])
                    ins.then_inc(S["tr_done"], 1)
                pe.wait_ge(S["T_act"], NTILE + n + 1)
                pe.wait_ge(S["T_dve"], NTILE + n + 1)
                if not first(n):
                    pe.wait_ge(S["logit_copied"], n)
                for k in range(KT):
                    ins = mm(SC[:, 0:NE], h2T[:, s, k, :], wr[:, k, :], start=k == 0, stop=k == KT - 1)
                ins.then_inc(S["logit_done"], 1)

            out_product(0, 0)
            out_product(1, 1)
            router(0, 0)
            with pe.Fori(1, NTILE // 2) as h:
                out_product(h * 2, 0)
                router(h * 2 - 1, 1)
                out_product(h * 2 + 1, 1)
                router(h * 2, 0)
            router(NTILE - 1, 1)

            pe.wait_ge(S["rank_mm"], 1)
            pe.wait_ge(S["patterns"], 16)
            mm(PJ[0][:, :], sut[:, :], lg[6][:, :], start=True, stop=True)
            mm(PJ[1][:, :], onesq[:, :], lg[6][:, :], start=True, stop=True).then_inc(S["rank_mm"], 1)
            pe.wait_ge(S["tbl_back"], 16)
            tr(SD[:, 0:NB], tblr[:, :], ident[0:NB, 0:NB]).then_inc(S["tbl_T"], 1)
            pe.wait_ge(S["idx_ready"], 1)

            GU, Y2, TX, TA = banks[0:2], banks[2:4], banks[4:6], banks[6]

            def rows_T(n, s):
                pe.wait_ge(SL["xg_in"][s], uses(n) * 16)
                for half in range(2):
                    if not first(n):
                        pe.wait_ge((S["T_act"], S["T_dve"])[half], 2 * NTILE + n)
                    for k in range(4):
                        kk_ = 4 * half + k
                        ins = tr(TX[half][:, k * P:k * P + P], xg[:, s, kk_ * P:kk_ * P + P], ident[:, :])
                    ins.then_inc(S["tr_done"], 1)

            def gate_up(n, s):
                pe.wait_ge(SL["we_in"][s], uses(n) * 32)
                pe.wait_ge(S["T_act"], 2 * NTILE + n + 1)
                pe.wait_ge(S["T_dve"], 2 * NTILE + n + 1)
                if not first(n):
                    pe.wait_ge(S["act_ready"], n)
                for j in range(2):
                    for k in range(KT):
                        ins = mm(GU[j][:, :], xT[:, s, k, :], WI[:, s, k, j * DE:j * DE + DE],
                                 start=k == 0, stop=k == KT - 1)
                ins.then_inc(S["gu_done"], 1)

            def act_T(n, s):
                pe.wait_ge(S["act_ready"], n + 1)
                if not first(n):
                    pe.wait_ge(S["actT_ready"], n)
                for k in range(4):
                    ins = tr(TA[:, k * P:k * P + P], actb[:, s, k * P:k * P + P], ident[:, :])
                ins.then_inc(S["actT_done"], 1)

            def down(n, s):
                pe.wait_ge(S["actT_ready"], n + 1)
                if not first(n):
                    pe.wait_ge(S["y_act"], n)
                    pe.wait_ge(S["y_dve"], n)
                for j in range(2):
                    for k in range(DE // P):
                        ins = mm(Y2[j][:, :], aT[:, s, k * P:k * P + P], WO[:, s, k, j * 512:j * 512 + 512],
                                 start=k == 0, stop=k == DE // P - 1)
                ins.then_inc(S["y2_done"], 1)

            rows_T(0, 0)
            gate_up(0, 0)
            rows_T(1, 1)
            act_T(0, 0)
            gate_up(1, 1)
            down(0, 0)
            with pe.Fori(1, NB // 2) as h:
                for s in range(2):
                    n = h * 2 + s
                    rows_T(n, s)
                    act_T(n - 1, 1 - s)
                    gate_up(n, s)
                    down(n - 1, 1 - s)
            act_T(NB - 1, 1)
            down(NB - 1, 1)

        @block.scalar
        def _(act):
            def fn(o, i, f, **kw):
                return nc.scalar.activation(o, i, f, **kw)

            act.wait_ge(S["par_ready"], 1)
            fn(csig[:, :], PT2[:, 10:18], ACT.Sigmoid).then_inc(S["c_sig"], 1)

            def norm_x(n, s):
                act.wait_ge(SL["x_in"][s], uses(n) * 16)
                if not first(n):
                    act.wait_ge(S["sumsq"], n)
                fn(xsq[:, :], xt[:, s], ACT.Square, accum_out=xst[:, s, 0:1]).then_inc(S["sumsq"], 1)
                act.wait_ge(S["sumsq"], n + 1)
                fn(xst[:, s, 1:2], xst[:, s, 0:1], ACT.Ln, scale=1.0 / D, bias=epsc[:, 0:1]).then_inc(S["ln_done"], 1)
                act.wait_ge(S["ln_done"], n + 1)
                fn(xst[:, s, 2:3], xst[:, s, 1:2], ACT.Exp, scale=-0.5).then_inc(S["rstd"], 1)

            def evac_x(n):
                act.wait_ge(S["tr_done"], n * 2 + 1)
                for k in range(4):
                    ins = fn(hT[:, k, ds(n * P, P)], PJ[0][:, k * P:k * P + P], ACT.Identity,
                             scale=modc[:, 0, k:k + 1], bias=modc[:, 1, k:k + 1])
                ins.then_inc(S["T_act"], 1)

            act.wait_ge(S["mod_ready"], 1)
            norm_x(0, 0)
            norm_x(1, 1)
            evac_x(0)
            with act.Fori(1, NTILE // 2) as h:
                for s in range(2):
                    norm_x(h * 2 + s, s)
                    evac_x(h * 2 + s - 1)
            evac_x(NTILE - 1)

            for g in range(NG):
                for m in range(2):
                    n = 2 * g + m
                    if g:
                        act.wait_ge(S["rank_mixed"], n - 1)
                        fn(rsc[:, m, 0:1], rsc[:, m, G:G + 1], ACT.Copy).then_inc(S["rank_carry"], 1)
                        act.wait_ge(S["rank_carry"], n - 1)
                    else:
                        act.wait_ge(S["cleared"], 2)
                    act.wait_ge(S["rank_done"], n + 1)
                    fn(rsc[:, m, 1:G + 1], (M0, M1)[m][:, :], ACT.Copy, scale=PT2[:, 8 + m:9 + m])\
                        .then_inc(S["rank_scaled"], 1)
                    act.wait_ge(S["rank_mixed"], n + 1)
                    if g:
                        act.wait_ge(S["rank_saved"], 32 * g)
                    if m == 0:
                        fn(rout[0:64, 0, :], rmx[0:64, 0, :], ACT.Tanh)
                        fn(rout[64:128, 0, :], rmx[64:128, 0, :], ACT.Copy).then_inc(S["rank_out"], 1)
                    else:
                        fn(rout[:, 1, :], rmx[:, 1, :], ACT.Sigmoid).then_inc(S["rank_out"], 1)

            def seq(q, c):
                act.wait_ge(S["x_done"], q * NC + c + 1)
                fn(xs[:, :], SA[:, 0:P], ACT.Copy, scale=-1.0).then_inc(S["x_copied"], 1)
                act.wait_ge(S["u_done"], q * NC + c + 1)
                fn(ut[:, :], SA[:, 0:P], ACT.Copy).then_inc(S["u_copied"], 1)

            def copy_y(q):
                act.wait_ge(S["y_done"], q * NC + NC)
                if not first(q):
                    act.wait_ge(S["merged_ready"], q)
                fn(yT[:, :], SC[:, :], ACT.Copy).then_inc(S["yT_copied"], 1)

            def centre(q):
                act.wait_ge(S["center_done"], q + 1)
                fn(yc[:, :], M1[:, :], ACT.Copy).then_inc(S["yc_step"], 1)
                fn(sq[:, :], M1[:, :], ACT.Square).then_inc(S["yc_step"], 1)

            def rstd(q):
                act.wait_ge(S["var_done"], q + 1)
                fn(rs[:, :], M0[:, :], ACT.Ln, scale=1.0 / HD, bias=epsc[:, 1:2]).then_inc(S["rs_step"], 1)
                act.wait_ge(S["rs_step"], q * 2 + 1)
                fn(rs[:, :], rs[:, :], ACT.Exp, scale=-0.5).then_inc(S["rs_step"], 1)

            def step(i, q):
                act.wait_ge(S["par_step"], i + 1)
                act.wait_ge(S["zdec_done"], i + 1)
                fn(sg[:, :], M0[:, :], ACT.Sigmoid, bias=par[:, Q_W0:Q_W0 + 1]).then_inc(S["sg_ready"], 1)
                act.wait_ge(S["zaaa_done"], i + 1)
                if not first(i):
                    act.wait_ge(S["b_ready"], i)
                fn(at[:, :], M1[:, :], ACT.Sigmoid, bias=par[:, Q_A0:Q_A0 + 1]).then_inc(S["a_ready"], 1)
                if not first(i):
                    act.wait_ge(S["shifted"], i * 3)
                fn(T3[:, :, 0:1], T3[:, :, G:G + 1], ACT.Copy, scale=nz[:, ds(group(i), 1)]).then_inc(S["carry_saved"], 1)
                act.wait_ge(S["carry_saved"], i + 1)

                def scaled(m, q_mu):
                    act.wait_ge(S["proj_done"], i * 8 + m + 1)
                    fn(T3[:, m, 1:G + 1], PJ[m % 2][:, :], ACT.Copy, scale=par[:, q_mu:q_mu + 1])\
                        .then_inc(S["shift_scaled"], 1)

                if q is not None:
                    seq(q, 0)
                    seq(q, 1)
                scaled(0, Q_MUK)
                act.wait_ge(S["shifted"], i * 3 + 1)
                if not first(i):
                    act.wait_ge(S["branch"], i * 3 - 2)
                fn(sq[:, :], kt[:, :], ACT.Square, scale=par[:, Q_KK:Q_KK + 1]).then_inc(S["ksq_ready"], 1)
                act.wait_ge(S["sgT_done"], i + 1)
                if not first(i):
                    act.wait_ge(S["operands"], i * 5)
                fn(sgT[:, :], M0[:, :], ACT.Copy).then_inc(S["sgT_copied"], 1)
                if q is not None:
                    seq(q, 2)
                    seq(q, 3)
                scaled(1, Q_MUR)
                act.wait_ge(S["cum_done"], i + 1)
                m1 = M1[:, :].rearrange("p (c t) -> p c t", t=C)
                if not first(i):
                    act.wait_ge(S["operands"], i * 5 - 2)
                    act.wait_ge(S["operands"], i * 5 - 3)
                    act.wait_ge(S["operands"], i * 5)
                fn(Pb[:, :, 1:C + 1], m1, ACT.Exp).then_inc(S["P_step"], 1)
                fn(Pinv[:, :], M1[:, :], ACT.Exp, scale=-1.0).then_inc(S["P_step"], 1)
                act.wait_ge(S["norm_max"], i + 1)
                fn(rn[:, :], rn[:, :], ACT.Ln, scale=TINY_SHIFT).then_inc(S["rn_step"], 1)
                act.wait_ge(S["rn_step"], i * 2 + 1)
                fn(rn[:, :], rn[:, :], ACT.Exp, scale=-0.5, bias=epsc[:, 2:3]).then_inc(S["rn_step"], 1)
                if q is not None:
                    seq(q, 4)
                    seq(q, 5)
                scaled(2, Q_MUV)
                act.wait_ge(S["shifted"], i * 3 + 3)
                if not first(i):
                    wait_gram(act, i - 1, ("TR", 0, 1, 0))
                v3 = vt[:, :].rearrange("p (c t) -> p c t", t=C)
                fn(Vb[0:64, :, 0:64], v3[0:64], ACT.Copy)
                fn(Vb[64:128, :, 64:128], v3[64:128], ACT.Copy).then_inc(S["V_written"], 1)
                if q is not None:
                    seq(q, 6)
                    seq(q, 7)
                    copy_y(q)
                act.wait_ge(S["proj_done"], i * 8 + 4)
                if not first(i):
                    act.wait_ge(S["branch"], i * 3 - 2)
                fn(chs[:, :], PJ[1][:, :], ACT.Copy).then_inc(S["ch_copied"], 1)
                if q is not None:
                    centre(q)
                    rstd(q)
                act.wait_ge(S["proj_done"], i * 8 + 7)
                act.wait_ge(S["u_made"], i + 1)
                fn(chs[:, :], PJ[0][:, :], ACT.Sigmoid).then_inc(S["gates"], 1)
                act.wait_ge(S["proj_done"], i * 8 + 8)
                if q is not None:
                    act.wait_ge(S["post_step"], q * 4 + 4)
                fn(gg[:, :], PJ[1][:, :], ACT.Sigmoid).then_inc(S["gates"], 1)
                for u in ON_ACT:
                    wait_gram(act, i, u)
                    _, m, b, _ = u
                    fn(tok[:, m, 4 * b:4 * b + 4, :], bank(u)[:, :].rearrange("p (c t) -> p c t", t=P), ACT.Copy)\
                        .then_inc(S["tok_copied"], 1)

            act.wait_ge(S["cleared"], 8)
            step(0, None)
            with act.Fori(1, STEPS) as i:
                step(i, i - 1)
            for c in range(NC):
                seq(STEPS - 1, c)
            copy_y(STEPS - 1)
            act.wait_ge(S["post_step"], STEPS * 4 - 7)
            centre(STEPS - 1)
            rstd(STEPS - 1)

            def norm2(n, s):
                act.wait_ge(S["x1_ready"], n + 1)
                if not first(n):
                    act.wait_ge(S["sumsq"], NTILE + n)
                fn(sq5[:, :], x1t[:, s], ACT.Square, accum_out=st5[:, s, 0:1]).then_inc(S["sumsq"], 1)
                act.wait_ge(S["sumsq"], NTILE + n + 1)
                fn(st5[:, s, 1:2], st5[:, s, 0:1], ACT.Ln, scale=1.0 / D, bias=epsc[:, 0:1]).then_inc(S["ln_done"], 1)
                act.wait_ge(S["ln_done"], NTILE + n + 1)
                fn(st5[:, s, 2:3], st5[:, s, 1:2], ACT.Exp, scale=-0.5).then_inc(S["rstd"], 1)

            def evac5(n, s):
                act.wait_ge(S["tr_done"], 2 * NTILE + n * 2 + 1)
                for k in range(4):
                    ins = fn(h2T[:, s, k, :], SA[:, k * P:k * P + P], ACT.Identity,
                             scale=modc[:, 2, k:k + 1], bias=modc[:, 3, k:k + 1])
                ins.then_inc(S["T_act"], 1)
                act.wait_ge(S["logit_done"], n + 1)
                fn(aff[:, ds(n * NE, NE)], SC[:, 0:NE], ACT.Copy).then_inc(S["logit_copied"], 1)

            norm2(0, 0)
            norm2(1, 1)
            evac5(0, 0)
            with act.Fori(1, NTILE // 2) as h:
                for s in range(2):
                    norm2(h * 2 + s, s)
                    evac5(h * 2 + s - 1, 1 - s)
            evac5(NTILE - 1, 1)
            act.wait_ge(S["logit_copied"], NTILE)
            fn(aff[:, :], aff[:, :], ACT.Sigmoid).then_inc(S["aff_ready"], 1)

            def xT_half(n, s):
                act.wait_ge(S["tr_done"], 4 * NTILE + n * 2 + 1)
                if not (isinstance(n, int) and n < 2):
                    act.wait_ge(S["gu_done"], n - 1)
                for k in range(4):
                    ins = fn(xT[:, s, k, :], banks[4][:, k * P:k * P + P], ACT.Identity,
                             scale=modc[:, 2, k:k + 1], bias=modc[:, 3, k:k + 1])
                ins.then_inc(S["T_act"], 1)

            def gate_sig(n, s):
                act.wait_ge(S["gu_done"], n + 1)
                fn(gsig[:, s], banks[0][:, :], ACT.Sigmoid).then_inc(S["sig_ready"], 1)

            def y_half(n, s):
                act.wait_ge(S["y2_done"], n + 1)
                if not (isinstance(n, int) and n < 2):
                    act.wait_ge(SL["y_out"][s], (n // 2) * 16)
                fn(ysb[:, s, 0:512], banks[2][:, :], ACT.Copy).then_inc(S["y_act"], 1)

            def actT(n, s):
                act.wait_ge(S["actT_done"], n + 1)
                if not (isinstance(n, int) and n < 2):
                    act.wait_ge(S["y2_done"], n - 1)
                fn(aT[:, s], banks[6][:, :], ACT.Copy).then_inc(S["actT_ready"], 1)

            act.wait_ge(S["idx_ready"], 1)
            xT_half(0, 0)
            gate_sig(0, 0)
            xT_half(1, 1)
            actT(0, 0)
            gate_sig(1, 1)
            y_half(0, 0)
            with act.Fori(1, NB // 2) as h:
                for s in range(2):
                    n = h * 2 + s
                    xT_half(n, s)
                    actT(n - 1, 1 - s)
                    gate_sig(n, s)
                    y_half(n - 1, 1 - s)
            actT(NB - 1, 1)
            y_half(NB - 1, 1)

            def tile8(n, s):
                act.wait_ge(SL["y8_in"][s], uses(n) * 32)
                if not (isinstance(n, int) and n < 2):
                    act.wait_ge(S["x2_ready"], n - 1)
                    act.wait_ge(S["o_ready"], n - 1)
                fn(c8[:, s], ya[:, s], ACT.Copy, scale=wts[:, 0, ds(n, 1)]).then_inc(S["y1w"], 1)
                act.wait_ge(S["x2_ready"], n + 1)
                if not first(n):
                    act.wait_ge(S["sumsq"], 2 * NTILE + n)
                fn(sq8[:, :], c8[:, s], ACT.Square, accum_out=st8[:, s, 0:1]).then_inc(S["sumsq"], 1)
                act.wait_ge(S["sumsq"], 2 * NTILE + n + 1)
                fn(st8[:, s, 1:2], st8[:, s, 0:1], ACT.Ln, scale=1.0 / D, bias=epsc[:, 0:1]).then_inc(S["ln_done"], 1)
                act.wait_ge(S["ln_done"], 2 * NTILE + n + 1)
                fn(st8[:, s, 2:3], st8[:, s, 1:2], ACT.Exp, scale=-0.5).then_inc(S["rstd"], 1)

            for s in range(2):
                act.wait_ge(SL["y_out"][s], 16 * NB // 2)
            pairs(act, tile8)

        @block.vector
        def _(dve):
            V = nc.vector
            links = [0]

            def link(ins):
                links[0] += 1
                ins.then_inc(S["chain"], 1)
                dve.wait_ge(S["chain"], links[0])

            V.memset(epsc[:, 0:1], EPS)
            V.memset(epsc[:, 1:2], LNX_EPS)
            V.memset(epsc[:, 2:3], 0.5 * math.log(TINY_SHIFT))
            V.memset(nz[:, 0:1], 0.0)
            V.memset(nz[:, 1:NG], 1.0)
            dve.wait_ge(S["patterns"], 5)
            dve.wait_ge(S["patterns"], 8)
            link(V.tensor_tensor(iop[:, :], iop[:, :], iof[:, :], ALU.bitwise_xor))
            link(V.tensor_copy(xr[:, :], iop[:, :]))
            link(V.tensor_tensor(lx[:, :], xr[:, :], low[:, :], ALU.mult))
            link(V.tensor_tensor(ux[:, :], xr[:, :], upp[:, :], ALU.mult))
            for lv in range(7):
                link(V.tensor_scalar(geq[:, lv, :], lx[:, :], float(2 ** lv), None, ALU.is_ge))
            for j, v in enumerate((1.0, 2.0, 64.0)):
                link(V.tensor_scalar(gequ[:, j, :], ux[:, :], v, None, ALU.is_ge))
            for lv in range(1, 6):
                link(V.tensor_tensor(mlev[:, lv - 1, :], geq[:, lv, :], geq[:, lv + 1, :], ALU.subtract))
            link(V.tensor_tensor(m0n[:, :], geq[:, 1, :], geq[:, 0, :], ALU.subtract))
            link(V.tensor_tensor(m0Tn[:, :], gequ[:, 1, :], gequ[:, 0, :], ALU.subtract))
            link(V.tensor_tensor(mN[:, 64:192], gequ[:, 0, :], gequ[:, 2, :], ALU.subtract))
            link(V.tensor_tensor(ux[:, :], mN[:, 64:192], ident[:, :], ALU.add))
            link(V.tensor_copy(mN[0:64, 0:64], ux[0:64, 0:64]))
            link(V.tensor_copy(mN[64:128, 0:64], ux[64:128, 64:128]))
            link(V.tensor_scalar(tri[:, :], ux[:, :], DECAY_SCALE, None, ALU.mult))
            link(V.tensor_scalar(ones_bd[:, :], xr[:, :], 64.0, None, ALU.is_lt))
            V.scalar_tensor_tensor(out=center[:, :], in0=ones_bd[:, :], scalar=-1.0 / HD, in1=ident[:, :],
                                   op0=ALU.mult, op1=ALU.add).then_inc(S["consts_ready"], 1)
            dve.wait_ge(S["par_T"], 1)
            link(V.tensor_copy(PT[:, 0:NLOAD, :], PJ[0][:, 0:112].rearrange("p (q c) -> p q c", c=KT)))
            link(V.tensor_copy(PT2[:, :], PJ[1][:, 0:18]))
            V.tensor_scalar(om2[:, :], PT2[:, 8:10], -1.0, 1.0, ALU.mult, ALU.add)
            V.tensor_scalar(PT[:, Q_OMR:Q_OMV + 1, :], PT[:, Q_MUR:Q_MUV + 1, :], -1.0, 1.0, ALU.mult, ALU.add)
            V.tensor_scalar(PT[:, Q_OKA, :], PT[:, Q_KA, :], -1.0, 1.0, ALU.mult, ALU.add).then_inc(S["par_ready"], 1)
            dve.wait_ge(S["c_sig"], 1)
            V.tensor_tensor(cond[:, :], csig[:, :], PT2[:, 10:18], ALU.mult).then_inc(S["cond_ready"], 1)
            dve.wait_ge(S["par_rows"], 288)
            for n in range(12):
                dve.wait_ge(S["ada_done"], n + 1)
                V.tensor_tensor(adarow[0:1, 512 * n:512 * n + 512], (M0, M1)[n % 2][0:1, :],
                                brow[0:1, 512 * n:512 * n + 512], ALU.add).then_inc(S["ada_row"], 1)
            dve.wait_ge(S["ada_T"], 1)
            link(V.tensor_copy(adaT[:, :], SA[:, 0:48]))
            link(V.tensor_scalar(modc[:, 0, :], adaT[:, 8:16], 1.0, None, ALU.add))
            link(V.tensor_tensor(modc[:, 0, :], modc[:, 0, :], PT[:, Q_N1, :], ALU.mult))
            link(V.tensor_copy(modc[:, 1, :], adaT[:, 0:8]))
            link(V.tensor_scalar(modc[:, 2, :], adaT[:, 32:40], 1.0, None, ALU.add))
            link(V.tensor_tensor(modc[:, 2, :], modc[:, 2, :], PT2[:, 0:8], ALU.mult))
            V.tensor_copy(modc[:, 3, :], adaT[:, 24:32]).then_inc(S["mod_ready"], 1)

            def scale_x(n, s):
                dve.wait_ge(S["rstd"], n + 1)
                V.tensor_scalar(xt[:, s], xt[:, s], xst[:, s, 2:3], None, ALU.mult).then_inc(S["xn_ready"], 1)

            def evac_x(n):
                dve.wait_ge(S["tr_done"], n * 2 + 2)
                for k in range(4):
                    ins = V.tensor_scalar(hT[:, 4 + k, ds(n * P, P)], PJ[1][:, k * P:k * P + P],
                                          modc[:, 0, 4 + k:5 + k], modc[:, 1, 4 + k:5 + k], ALU.mult, ALU.add)
                ins.then_inc(S["T_dve"], 1)

            dve.wait_ge(S["mod_ready"], 1)
            scale_x(0, 0)
            scale_x(1, 1)
            evac_x(0)
            with dve.Fori(1, NTILE // 2) as h:
                for s in range(2):
                    scale_x(h * 2 + s, s)
                    evac_x(h * 2 + s - 1)
            evac_x(NTILE - 1)

            dve.wait_ge(S["tr_done"], 2 * NTILE)
            V.memset(rsc[:, 0, 0:1], 0.0).then_inc(S["cleared"], 1)
            V.memset(rsc[:, 1, 0:1], 0.0).then_inc(S["cleared"], 1)
            for n in range(2 * NG):
                m = n % 2
                dve.wait_ge(S["rank_scaled"], n + 1)
                if n >= 2:
                    dve.wait_ge(S["rank_out"], n - 1)
                V.scalar_tensor_tensor(out=rmx[:, m], in0=(M0, M1)[m][:, :], scalar=om2[:, m:m + 1],
                                       in1=rsc[:, m, 0:G], op0=ALU.mult, op1=ALU.add).then_inc(S["rank_mixed"], 1)

            dve.wait_ge(S["rank_saved"], 32 * NG)
            V.memset(UP[64:128, 0, :], 0.0)
            V.memset(UP[0:64, 1, :], 0.0).then_inc(S["cleared"], 1)
            V.memset(T3[:, :, :], 0.0)
            V.memset(Pb[:, :, 0:1], 1.0).then_inc(S["cleared"], 1)
            V.memset(AR[0:64, :, 128:192], 0.0)
            V.memset(AR[64:128, :, 64:128], 0.0).then_inc(S["cleared"], 1)
            for m in (Bb, Kb, Vb):
                V.memset(m[0:64, :, 64:128], 0.0)
                ins = V.memset(m[64:128, :, 0:64], 0.0)
            ins.then_inc(S["cleared"], 1)
            V.memset(St[:, :, :], 0.0).then_inc(S["cleared"], 1)
            V.memset(ub[:, :], 0.0).then_inc(S["cleared"], 1)

            def half(t, h):
                return t[64 * h:64 * h + 64]

            def S_update(q, c):
                dve.wait_ge(S["s_done"], q * NC + c + 1)
                if c:
                    dve.wait_ge(S["S_updated"], q * NC + c)
                V.scalar_tensor_tensor(out=St[:, (c + 1) % 2, :], in0=St[:, c % 2, :], scalar=pcs[:, c:c + 1],
                                       in1=SB[:, 0:P], op0=ALU.mult, op1=ALU.add).then_inc(S["S_updated"], 1)

            def post(q):
                dve.wait_ge(S["rs_step"], q * 2 + 2)
                dve.wait_ge(S["yc_step"], q * 2 + 1)
                V.tensor_tensor(yc[:, :], yc[:, :], rs[:, :], ALU.mult).then_inc(S["post_step"], 1)
                dve.wait_ge(S["post_step"], q * 4 + 1)
                V.tensor_scalar(yc[:, :], yc[:, :], parQ[:, Q_LNW:Q_LNW + 1], parQ[:, Q_LNB:Q_LNB + 1],
                                ALU.mult, ALU.add).then_inc(S["post_step"], 1)
                dve.wait_ge(S["post_step"], q * 4 + 2)
                V.tensor_tensor(yc[:, :], yc[:, :], bv[:, :], ALU.add).then_inc(S["post_step"], 1)
                dve.wait_ge(S["post_step"], q * 4 + 3)
                V.tensor_tensor(yc[:, :], yc[:, :], gg[:, :], ALU.mult).then_inc(S["post_step"], 1)
                dve.wait_ge(S["post_step"], q * 4 + 4)
                if not first(q):
                    dve.wait_ge(S["merged_out"], q * 16)
                V.tensor_tensor(mg[:, :], yc[:, :], conv[:, :], ALU.add).then_inc(S["merged_ready"], 1)

            def mixed(i, m, t, q_om):
                dve.wait_ge(S["shift_scaled"], i * 3 + m + 1)
                V.scalar_tensor_tensor(out=t[:, :], in0=PJ[m % 2][:, :], scalar=par[:, q_om:q_om + 1],
                                       in1=T3[:, m, 0:G], op0=ALU.mult, op1=ALU.add).then_inc(S["shifted"], 1)

            def start_seq(q):
                if not first(q):
                    dve.wait_ge(S["S_updated"], q * NC)
                V.tensor_scalar(St[:, 0, :], St[:, 0, :], nz[:, ds(group(q), 1)], None, ALU.mult)\
                    .then_inc(S["S_init"], 1)
                dve.wait_ge(S["S_init"], q + 1)

            def step(i, q):
                if q is not None:
                    dve.wait_ge(S["par_step"], i)
                    V.tensor_copy(parQ[:, :], par[:, :]).then_inc(S["parq_step"], 1)
                    dve.wait_ge(S["parq_step"], i)
                    dve.wait_ge(S["gates"], i * 2)
                V.tensor_copy(par[:, :], PT[:, :, ds(i // NG, 1)].rearrange("p a b -> p (a b)"))\
                    .then_inc(S["par_step"], 1)
                dve.wait_ge(S["par_step"], i + 1)
                if not first(i):
                    dve.wait_ge(S["bonus_done"], i)
                V.tensor_scalar(rkbd[:, :], ones_bd[:, :], par[:, Q_RK:Q_RK + 1], None, ALU.mult)\
                    .then_inc(S["rkbd_ready"], 1)
                if q is not None:
                    start_seq(q)
                    S_update(q, 0)
                    S_update(q, 1)
                mixed(i, 0, kt, Q_OMK)
                dve.wait_ge(S["a_ready"], i + 1)
                V.tensor_scalar(km[:, :], at[:, :], par[:, Q_KA:Q_KA + 1], par[:, Q_OKA:Q_OKA + 1],
                                ALU.mult, ALU.add).then_inc(S["km_step"], 1)
                dve.wait_ge(S["km_step"], i * 2 + 1)
                dve.wait_ge(S["shifted"], i * 3 + 1)
                V.tensor_tensor(km[:, :], km[:, :], kt[:, :], ALU.mult).then_inc(S["km_step"], 1)
                if q is not None:
                    S_update(q, 2)
                    S_update(q, 3)
                mixed(i, 1, rt, Q_OMR)
                dve.wait_ge(S["norm_done"], i + 1)
                V.tensor_scalar(rn[:, :], M0[:, :], 1e-24, None, ALU.max).then_inc(S["norm_max"], 1)
                dve.wait_ge(S["shifted"], i * 3 + 2)
                dve.wait_ge(S["km_step"], i * 2 + 2)
                dve.wait_ge(S["sgT_done"], i + 1)
                V.tensor_tensor(rk[:, :], rt[:, :], km[:, :], ALU.mult).then_inc(S["rk_ready"], 1)
                if q is not None:
                    S_update(q, 4)
                    S_update(q, 5)
                dve.wait_ge(S["rn_step"], i * 2 + 2)
                V.scalar_tensor_tensor(out=kk[:, :], in0=kt[:, :], scalar=par[:, Q_KK:Q_KK + 1], in1=rn[:, :],
                                       op0=ALU.mult, op1=ALU.mult).then_inc(S["kk_ready"], 1)
                mixed(i, 2, vt, Q_OMV)
                if q is not None:
                    S_update(q, 6)
                    S_update(q, 7)
                    dve.wait_ge(S["y_done"], i * NC)
                    dve.wait_ge(S["S_updated"], i * NC)
                dve.wait_ge(S["P_step"], i * 2 + 1)
                dve.wait_ge(S["kk_ready"], i + 1)

                def c3(t):
                    return t[:, :].rearrange("p (c t) -> p c t", t=C)

                V.tensor_tensor(AR[:, :, 0:64], c3(rt), Pb[:, :, 1:C + 1], ALU.mult).then_inc(S["operands"], 1)
                V.tensor_copy(pcs[:, :], Pb[:, :, C:C + 1].rearrange("p c o -> p (c o)")).then_inc(S["operands"], 1)
                for h in range(2):
                    ins = V.tensor_tensor(half(AR, h)[:, :, 64 + 64 * h:128 + 64 * h], half(c3(kk), h),
                                          half(Pb, h)[:, :, 0:C], ALU.mult)
                ins.then_inc(S["operands"], 1)
                dve.wait_ge(S["operands"], i * 5 + 3)
                V.tensor_tensor(kk[:, :], kk[:, :], at[:, :], ALU.mult).then_inc(S["b_ready"], 1)
                dve.wait_ge(S["P_step"], i * 2 + 2)
                dve.wait_ge(S["b_ready"], i + 1)
                for h in range(2):
                    ins = V.tensor_tensor(half(Bb, h)[:, :, 64 * h:64 * h + 64], half(c3(kk), h),
                                          half(c3(Pinv), h), ALU.mult)
                ins.then_inc(S["operands"], 1)
                for h in range(2):
                    ins = V.tensor_tensor(half(Kb, h)[:, :, 64 * h:64 * h + 64], half(c3(km), h),
                                          half(c3(Pinv), h), ALU.mult)
                ins.then_inc(S["operands"], 1)
                if not first(i):
                    dve.wait_ge(S["u_made"], i)
                V.tensor_scalar(ub[:, 0:2], ub[:, G:G + 2], nz[:, ds(group(i), 1)], None, ALU.mult)\
                    .then_inc(S["u_carry"], 1)
                dve.wait_ge(S["u_carry"], i + 1)
                dve.wait_ge(S["ch_copied"], i + 1)
                dve.wait_ge(S["proj_done"], i * 8 + 5)
                V.tensor_tensor(ub[:, 2:G + 2], PJ[0][:, :], chs[:, :], ALU.mult).then_inc(S["u_made"], 1)
                dve.wait_ge(S["u_made"], i + 1)
                V.tensor_scalar(cg[:, :], ub[:, 0:G], par[:, Q_CW0:Q_CW0 + 1], None, ALU.mult).then_inc(S["conv_step"], 1)
                dve.wait_ge(S["conv_step"], i * 3 + 1)
                V.scalar_tensor_tensor(out=cg[:, :], in0=ub[:, 1:G + 1], scalar=par[:, Q_CW1:Q_CW1 + 1],
                                       in1=cg[:, :], op0=ALU.mult, op1=ALU.add).then_inc(S["conv_step"], 1)
                dve.wait_ge(S["conv_step"], i * 3 + 2)
                V.scalar_tensor_tensor(out=cg[:, :], in0=ub[:, 2:G + 2], scalar=par[:, Q_CW2:Q_CW2 + 1],
                                       in1=cg[:, :], op0=ALU.mult, op1=ALU.add).then_inc(S["conv_step"], 1)
                dve.wait_ge(S["conv_step"], i * 3 + 3)
                dve.wait_ge(S["proj_done"], i * 8 + 6)
                V.tensor_tensor(cg[:, :], PJ[1][:, :], cg[:, :], ALU.mult).then_inc(S["cb_gated"], 1)
                if q is not None:
                    post(q)
                    dve.wait_ge(S["merged_ready"], i)
                dve.wait_ge(S["cb_gated"], i + 1)
                dve.wait_ge(S["gates"], i * 2 + 1)
                V.tensor_tensor(conv[:, :], cg[:, :], chs[:, :], ALU.mult).then_inc(S["branch"], 1)
                dve.wait_ge(S["gates"], i * 2 + 2)
                dve.wait_ge(S["gup_done"], i + 1)
                V.tensor_tensor(gg[:, :], M1[:, :], gg[:, :], ALU.mult).then_inc(S["branch"], 1)
                dve.wait_ge(S["bonus_done"], i + 1)
                V.tensor_tensor(bv[:, :], M0[:, :], vt[:, :], ALU.mult).then_inc(S["branch"], 1)
                for u in ON_DVE:
                    kind, lv, b, h = u
                    wait_gram(dve, i, u)
                    bk = bank(u)[:, :].rearrange("p (c t) -> p c t", t=P)
                    cs = slice(4 * b, 4 * b + 4)

                    def over(m, n=4):
                        return m.unsqueeze(1).to_broadcast([P, n, m.shape[1]])

                    if kind == "L":
                        ins = V.tensor_tensor(Tm[:, cs, :], bk, over(m0n[:, :]), ALU.mult)
                    elif kind in ("LT", "GK"):
                        c = 4 * b + 2 * h
                        ins = V.tensor_tensor((LTb if kind == "LT" else GKb)[:, c:c + 2, :],
                                              bank(u)[:, 0:384].rearrange("p (c t) -> p c t", t=192),
                                              over(mN[:, :], 2), ALU.mult)
                    elif kind == "Z":
                        ins = V.tensor_tensor(Zm[:, cs, :], bk, over(mlev[:, lv - 1, :]), ALU.mult)
                    elif kind == "T":
                        ins = V.tensor_tensor(Tm[:, cs, :], Tm[:, cs, :], bk, ALU.subtract)
                    else:
                        ins = V.tensor_tensor(Qm[:, cs, :], Qm[:, cs, :], bk, ALU.subtract)
                    ins.then_inc(S["gram_evac"], 1)
                    if kind == "L":
                        wait_evac(dve, i, u)
                        V.tensor_tensor(Tm[:, cs, :], Tm[:, cs, :], over(ident[:, :]), ALU.add)\
                            .then_inc(S["T_seeded"], 1)
                    if kind == "LT" and h == 1:
                        wait_evac(dve, i, u)
                        V.tensor_tensor(Qm[:, cs, :], LTb[:, cs, 64:192], over(m0Tn[:, :]), ALU.mult)\
                            .then_inc(S["Q_half"], 1)
                        dve.wait_ge(S["Q_half"], i * 2 + b + 1)
                        V.tensor_tensor(Qm[:, cs, :], Qm[:, cs, :], over(ident[:, :]), ALU.add)\
                            .then_inc(S["Q_seeded"], 1)
                    if u == ("Q", 1, 1, 0):
                        dve.wait_ge(S["operands"], i * 5 + 2)
                        dve.wait_ge(S["operands"], i * 5 + 4)
                        V.tensor_tensor(Bb[:, :, :], Bb[:, :, :],
                                        pcs[:, :].unsqueeze(2).to_broadcast([P, NC, P]), ALU.mult)\
                            .then_inc(S["hats"], 1)
                    if u == ("Q", 2, 1, 0):
                        dve.wait_ge(S["operands"], i * 5 + 5)
                        V.tensor_tensor(Kb[:, :, :], Kb[:, :, :],
                                        pcs[:, :].unsqueeze(2).to_broadcast([P, NC, P]), ALU.mult)\
                            .then_inc(S["hats"], 1)

            step(0, None)
            with dve.Fori(1, STEPS) as i:
                step(i, i - 1)
            link(V.tensor_copy(parQ[:, :], par[:, :]))
            start_seq(STEPS - 1)
            for c in range(NC):
                S_update(STEPS - 1, c)
            dve.wait_ge(S["branch"], STEPS * 3 - 2)
            dve.wait_ge(S["branch"], STEPS * 3 - 1)
            dve.wait_ge(S["branch"], STEPS * 3)
            post(STEPS - 1)

            V.memset(ones_row[0:1, :], 1.0).then_inc(S["cleared"], 1)
            for n in range(7):
                dve.wait_ge(S["bcast_done"], n + 1)
                dst = [g1b, g1b, g2b, g2b, fgb, fgb, biasb][n]
                wd, at_ = (512, 512 * (n % 2)) if n < 6 else (NE, 0)
                V.tensor_copy(dst[:, at_:at_ + wd], PJ[n % 2][:, 0:wd]).then_inc(S["bcast_ready"], 1)
            dve.wait_ge(S["bcast_ready"], 7)

            def residual(n, s):
                dve.wait_ge(S["mix_done"], n + 1)
                if not (isinstance(n, int) and n < 2):
                    dve.wait_ge(SL["x1_out"][s], (n // 2) * 16)
                    dve.wait_ge(S["sumsq"], NTILE + n - 1)
                    dve.wait_ge(S["xn2_ready"], n - 1)
                for j in range(2):
                    ins = V.tensor_tensor(x1t[:, s, 512 * j:512 * j + 512], banks[2 * s + j][:, :],
                                          g1b[:, 512 * j:512 * j + 512], ALU.mult)
                ins.then_inc(S["mixed"], 1)
                dve.wait_ge(S["mixed"], n + 1)
                dve.wait_ge(SL["x5_in"][s], uses(n) * 16)
                V.tensor_tensor(x1t[:, s], x1t[:, s], x5[:, s], ALU.add).then_inc(S["x1_ready"], 1)

            def scale5(n, s):
                dve.wait_ge(S["rstd"], NTILE + n + 1)
                if not (isinstance(n, int) and n < 2):
                    dve.wait_ge(S["tr_done"], 2 * NTILE + (n - 1) * 2)
                    dve.wait_ge(SL["xn2_out"][s], (n // 2) * 16)
                V.tensor_scalar(xn2[:, s], x1t[:, s], st5[:, s, 2:3], None, ALU.mult).then_inc(S["xn2_ready"], 1)

            def evac5(n, s):
                dve.wait_ge(S["tr_done"], 2 * NTILE + n * 2 + 2)
                for k in range(4):
                    ins = V.tensor_scalar(h2T[:, s, 4 + k, :], SB[:, k * P:k * P + P], modc[:, 2, 4 + k:5 + k],
                                          modc[:, 3, 4 + k:5 + k], ALU.mult, ALU.add)
                ins.then_inc(S["T_dve"], 1)

            residual(0, 0)
            scale5(0, 0)
            residual(1, 1)
            scale5(1, 1)
            evac5(0, 0)
            with dve.Fori(1, NTILE // 2) as h:
                for s in range(2):
                    residual(h * 2 + s, s)
                    scale5(h * 2 + s, s)
                    evac5(h * 2 + s - 1, 1 - s)
            evac5(NTILE - 1, 1)

            dve.wait_ge(S["aff_ready"], 1)
            dve.wait_ge(S["patterns"], 16)
            for s in range(2):
                dve.wait_ge(SL["xn2_out"][s], 16 * NTILE // 2)
                dve.wait_ge(SL["x1_out"][s], 16 * NTILE // 2)
            TT, TS, RED = V.tensor_tensor, V.tensor_scalar, V.tensor_reduce
            (sel, masked, eq, oh1, oh2, tmp, both, rank, tot, posn) = lg

            def e3(t):
                return t[:, :].rearrange("p (n e) -> p n e", e=NE)

            def g3(t):
                return t[:, :].rearrange("p (n g) -> p n g", g=NGRP)

            def pick(t, m):
                return t[:, :].rearrange("p (x m) -> p x m", m=EPG)[:, :, m]

            def bc(t, k):
                return t.unsqueeze(2).to_broadcast([P, t.shape[1], k])

            link(TT(e3(sel), e3(aff), biasb[:, :].unsqueeze(1).to_broadcast([P, NTILE, NE]), ALU.add))
            for d, a, b, op in ((0, 0, 1, ALU.max), (1, 0, 1, ALU.min), (2, 2, 3, ALU.max), (3, 2, 3, ALU.min)):
                link(TT(s8[d][:, :], pick(sel, a), pick(sel, b), op))
            link(TT(s8[4][:, :], s8[0][:, :], s8[2][:, :], ALU.max))
            link(TT(s8[5][:, :], s8[0][:, :], s8[2][:, :], ALU.min))
            link(TT(s8[6][:, :], s8[1][:, :], s8[3][:, :], ALU.max))
            link(TT(s8[5][:, :], s8[5][:, :], s8[6][:, :], ALU.max))
            link(TT(s8[4][:, :], s8[4][:, :], s8[5][:, :], ALU.add))
            link(RED(s16[0][:, :], g3(s8[4]), AX.X, ALU.max))
            link(TT(g3(s8[5]), g3(s8[4]), bc(s16[0][:, :], NGRP), ALU.is_equal))
            link(TT(s8[5][:, :], s8[5][:, :], revg[:, :], ALU.mult))
            link(RED(s16[0][:, :], g3(s8[5]), AX.X, ALU.max))
            link(TT(g3(s8[6]), g3(s8[5]), bc(s16[0][:, :], NGRP), ALU.is_equal))
            link(TS(s8[7][:, :], s8[6][:, :], 3e38, -3e38, ALU.mult, ALU.add))
            grp = sel[:, :].rearrange("p (x m) -> p x m", m=EPG)
            msk = masked[:, :].rearrange("p (x m) -> p x m", m=EPG)
            link(TT(msk, grp, bc(s8[6][:, :], EPG), ALU.mult))
            link(TT(msk, msk, bc(s8[7][:, :], EPG), ALU.add))
            for j, oh in ((0, oh1), (1, oh2)):
                link(RED(s16[1][:, :], e3(masked), AX.X, ALU.max))
                link(TT(e3(eq), e3(masked), bc(s16[1][:, :], NE), ALU.is_equal))
                link(TT(eq[:, :], eq[:, :], reve[:, :], ALU.mult))
                link(RED(s16[1][:, :], e3(eq), AX.X, ALU.max))
                link(TT(e3(oh), e3(eq), bc(s16[1][:, :], NE), ALU.is_equal))
                link(TT(tmp[:, :], oh[:, :], aff[:, :], ALU.mult))
                link(RED(s16[2 + j][:, :], e3(tmp), AX.X, ALU.add))
                if j == 0:
                    link(TS(tmp[:, :], oh[:, :], -3e38, None, ALU.mult))
                    link(TT(masked[:, :], masked[:, :], tmp[:, :], ALU.add))
            link(TT(s16[4][:, :], s16[2][:, :], s16[3][:, :], ALU.add))
            link(V.reciprocal(s16[5][:, :], s16[4][:, :]))
            link(TT(wts[:, 0, :], s16[2][:, :], s16[5][:, :], ALU.mult))
            link(TT(wts[:, 1, :], s16[3][:, :], s16[5][:, :], ALU.mult))
            TT(both[:, :], oh1[:, :], oh2[:, :], ALU.add).then_inc(S["rank_mm"], 1)
            dve.wait_ge(S["rank_mm"], 2)
            link(V.tensor_copy(rank[:, :], PJ[0][:, :]))
            link(V.tensor_copy(tot[:, :], PJ[1][:, :]))
            for n in range(1, NTILE):
                link(TT(tot[:, n * NE:n * NE + NE], tot[:, n * NE:n * NE + NE], tot[:, n * NE - NE:n * NE], ALU.add))
            link(TT(rank[:, NE:], rank[:, NE:], tot[:, 0:RW - NE], ALU.add))
            size = tot[:, RW - NE:]
            link(TS(e32[0][:, 0:NE], size, float(P - 1), None, ALU.add))
            link(V.tensor_copy(e32i[:, :], e32[0][:, 0:NE]))
            link(TS(e32i[:, :], e32i[:, :], 7, None, ALU.arith_shift_right))
            link(V.memset(e32[1][:, 0:32], 0.0))
            link(V.tensor_copy(e32[1][:, 32:64], e32i[:, :]))
            link(V.memset(e32[2][:, 0:32], 0.0))
            src, dst = e32[1], e32[2]
            for sh in (1, 2, 4, 8, 16):
                link(TT(dst[:, 32:64], src[:, 32:64], src[:, 32 - sh:64 - sh], ALU.add))
                src, dst = dst, src
            link(TS(e32[3][:, 0:NE], src[:, 31:63], float(P), None, ALU.mult))
            link(TT(e3(posn), e3(rank), e32[3][:, 0:NE].unsqueeze(1).to_broadcast([P, NTILE, NE]), ALU.add))
            for j, oh in ((0, oh1), (1, oh2)):
                link(TT(tmp[:, :], posn[:, :], oh[:, :], ALU.mult))
                link(RED(s16[j][:, :], e3(tmp), AX.X, ALU.add))
                link(V.tensor_copy(dest[:, j, :], s16[j][:, :]))
            V.tensor_copy(e32[4][0:1, 0:1], s16[0][0:1, 0:1]).then_inc(S["dest_ready"], 1)
            link(TT(bcmp[0:1, :, :], bidx[0:1, :, :], src[0:1, 32:64].unsqueeze(1).to_broadcast([1, NB, NE]),
                     ALU.is_ge))
            link(RED(bf[0:1, :], bcmp[0:1, :, :], AX.X, ALU.add))
            link(TS(bf[0:1, :], bf[0:1, :], float(NE - 1), None, ALU.min))
            V.tensor_copy(blk[0:1, :], bf[0:1, :]).then_inc(S["blk_ready"], 1)
            dve.wait_ge(S["tbl_T"], 1)
            V.tensor_copy(IDX[:, :], SD[:, 0:NB]).then_inc(S["idx_ready"], 1)

            def xT_half(n, s):
                dve.wait_ge(S["tr_done"], 4 * NTILE + n * 2 + 2)
                if not (isinstance(n, int) and n < 2):
                    dve.wait_ge(S["gu_done"], n - 1)
                for k in range(4):
                    ins = V.tensor_scalar(xT[:, s, 4 + k, :], banks[5][:, k * P:k * P + P],
                                          modc[:, 2, 4 + k:5 + k], modc[:, 3, 4 + k:5 + k], ALU.mult, ALU.add)
                ins.then_inc(S["T_dve"], 1)

            def swiglu(n, s):
                dve.wait_ge(S["sig_ready"], n + 1)
                V.tensor_tensor(gsig[:, s], banks[0][:, :], gsig[:, s], ALU.mult).then_inc(S["silu_ready"], 1)
                dve.wait_ge(S["silu_ready"], n + 1)
                if not (isinstance(n, int) and n < 2):
                    dve.wait_ge(S["actT_done"], n - 1)
                V.tensor_tensor(actb[:, s], banks[1][:, :], gsig[:, s], ALU.mult).then_inc(S["act_ready"], 1)

            def y_half(n, s):
                dve.wait_ge(S["y2_done"], n + 1)
                if not (isinstance(n, int) and n < 2):
                    dve.wait_ge(SL["y_out"][s], (n // 2) * 16)
                V.tensor_copy(ysb[:, s, 512:1024], banks[3][:, :]).then_inc(S["y_dve"], 1)

            xT_half(0, 0)
            swiglu(0, 0)
            xT_half(1, 1)
            swiglu(1, 1)
            y_half(0, 0)
            with dve.Fori(1, NB // 2) as h:
                for s in range(2):
                    n = h * 2 + s
                    xT_half(n, s)
                    swiglu(n, s)
                    y_half(n - 1, 1 - s)
            y_half(NB - 1, 1)

            for s in range(2):
                dve.wait_ge(SL["y_out"][s], 16 * NB // 2)

            def tile8(n, s):
                dve.wait_ge(S["y1w"], n + 1)
                V.scalar_tensor_tensor(out=c8[:, s], in0=yb[:, s], scalar=wts[:, 1, ds(n, 1)], in1=c8[:, s],
                                       op0=ALU.mult, op1=ALU.add).then_inc(S["y12"], 1)
                dve.wait_ge(S["y12"], n + 1)
                V.tensor_tensor(c8[:, s], c8[:, s], g2b[:, :], ALU.mult).then_inc(S["y12g"], 1)
                dve.wait_ge(S["y12g"], n + 1)
                dve.wait_ge(SL["x8_in"][s], uses(n) * 16)
                V.tensor_tensor(c8[:, s], c8[:, s], x8[:, s], ALU.add).then_inc(S["x2_ready"], 1)

            def out8(n, s):
                dve.wait_ge(S["rstd"], 2 * NTILE + n + 1)
                if not (isinstance(n, int) and n < 2):
                    dve.wait_ge(SL["o_out"][s], (n // 2) * 16)
                V.scalar_tensor_tensor(out=o8[:, s], in0=c8[:, s], scalar=st8[:, s, 2:3], in1=fgb[:, :],
                                       op0=ALU.mult, op1=ALU.mult).then_inc(S["o_ready"], 1)

            tile8(0, 0)
            tile8(1, 1)
            out8(0, 0)
            with dve.Fori(1, NTILE // 2) as h:
                for s in range(2):
                    tile8(h * 2 + s, s)
                    out8(h * 2 + s - 1, 1 - s)
            out8(NTILE - 1, 1)


_INS = ['x', 'c', 'w_ada', 'b_ada', 'norm1_gain', 'norm2_gain', 'w_in', 'token_mu', 'conv_w', 'w0', 'decay_up', 'a0',
        'aaa_up', 'gate_up', 'k_k', 'k_a', 'r_k', 'ln_x_w', 'ln_x_b', 'w_out', 'w_router', 'router_bias',
        'w_expert_in', 'w_expert_out', 'final_gain']


def kernel(**inputs):
    import numpy as _np
    import concourse.bacc as _bacc
    from concourse import mybir as _mybir
    from concourse.bass_utils import run_bass_kernel_spmd as _run

    nc = _bacc.Bacc("TRN2", target_bir_lowering=False, num_devices=1)
    arrays, io = {}, {}
    for name in _INS:
        a = _np.ascontiguousarray(inputs[name])
        arrays[f"in_{name}_dram"] = a
        io[name] = nc.dram_tensor(f"in_{name}_dram", a.shape, _mybir.dt.from_np(a.dtype), kind="ExternalInput").ap()
    out = nc.dram_tensor("out_0_dram", (1, T, D), F32, kind="ExternalOutput").ap()
    build(nc, io, out)
    r = _run(nc, [arrays], core_ids=[0])
    return r.results[0]["out_0_dram"]
```
